# Optimizing a Trainium2 kernel written in Bass

```python
import math
import jax
import jax.numpy as jnp
from jax import lax
import numpy as np

D_MODEL = 2048
BATCH = 1
SEQ = 256
DEPTH = 1

GRID_W = 64
CTX_LEN = 256
N_MIXERS = 3
N_LAYERS_A = (DEPTH + 2) // N_MIXERS
N_LAYERS_B = (DEPTH + 1) // N_MIXERS
N_LAYERS_C = DEPTH // N_MIXERS
NORM_EPS = 1e-6
ROPE_THETA = 10000.0

SSM_D_INNER = 2 * D_MODEL
SSM_HEAD_DIM = 64
SSM_HEADS = SSM_D_INNER // SSM_HEAD_DIM
SSM_STATE = 128
SSM_GROUPS = 8
SSM_CONV = 3
SSM_CHUNK = 128
SSM_CONV_DIM = SSM_D_INNER + 2 * SSM_GROUPS * SSM_STATE
SSM_IN_DIM = SSM_D_INNER + SSM_CONV_DIM + 2 * SSM_HEADS

HEAD_DIM = 128
WIN_HEADS = D_MODEL // HEAD_DIM
WIN_KV_HEADS = 4
WINDOW = 128
BLOCK = 128
DIFF_HEADS = D_MODEL // (2 * HEAD_DIM)

MOE_GROUPS = 4
MOE_EXPERTS_PER_GROUP = 8
MOE_EXPERTS = MOE_GROUPS * MOE_EXPERTS_PER_GROUP
MOE_TOP_K = 2
MOE_D_FF = D_MODEL // 4
MOE_BLOCK = 128

F32 = jnp.float32

kernel_name = "hybrid_ssd_swa_diffattn_hmoe_dit"

def rms_norm(x, gain):
    xf = x.astype(F32)
    y = xf * lax.rsqrt(jnp.mean(xf * xf, axis=-1, keepdims=True) + NORM_EPS)
    return (y * gain.astype(F32)).astype(x.dtype)

def modulate(h, shift, scale):
    return h * (1.0 + scale) + shift

def modulation(cvec, w, b):
    return jnp.split(jax.nn.silu(cvec) @ w + b, 6, axis=-1)

def axial_rope(n_tokens, head_dim):
    rows = n_tokens // GRID_W
    pos = jnp.arange(rows * GRID_W)
    row = (pos // GRID_W).astype(F32)
    col = (pos % GRID_W).astype(F32)
    quarter = head_dim // 4
    inv_freq = ROPE_THETA ** (-jnp.arange(quarter, dtype=F32) / quarter)
    ang = jnp.stack([row[:, None] * inv_freq, col[:, None] * inv_freq], axis=1)
    return jnp.cos(ang), jnp.sin(ang)

def apply_rope(x, cos, sin):
    b, s, h, d = x.shape
    xr = x.astype(F32).reshape(b, s, h, 2, 2, d // 4)
    x1, x2 = xr[..., 0, :], xr[..., 1, :]
    cs, sn = cos[None, :, None], sin[None, :, None]
    out = jnp.stack([x1 * cs - x2 * sn, x2 * cs + x1 * sn], axis=-2)
    return out.reshape(b, s, h, d).astype(x.dtype)

def centred_dwconv(u, w, bias):
    out = lax.conv_general_dilated(
        u, w[:, None, :].astype(u.dtype), window_strides=(1,),
        padding=[(SSM_CONV // 2, SSM_CONV // 2)],
        dimension_numbers=("NWC", "WIO", "NWC"), feature_group_count=u.shape[-1])
    return out + bias

def ssd_scan(xs, dt, a, bm, cm, h0):
    b, l, h, p = xs.shape
    nc = l // SSM_CHUNK
    r = h // SSM_GROUPS

    def chunks(t, *tail):
        return jnp.moveaxis(t.astype(F32).reshape(b, nc, SSM_CHUNK, *tail), 1, 0)

    xq = chunks(xs, SSM_GROUPS, r, p)
    laq = chunks(dt * a, SSM_GROUPS, r)
    dtq = chunks(dt, SSM_GROUPS, r)
    bq = chunks(bm, SSM_GROUPS, SSM_STATE)
    cq = chunks(cm, SSM_GROUPS, SSM_STATE)
    tri = jnp.tril(jnp.ones((SSM_CHUNK, SSM_CHUNK), dtype=bool))

    def step(state, inp):
        x_, la, dt_, b_, c_ = inp
        cum = jnp.moveaxis(jnp.cumsum(la, axis=1), 1, -1)
        seg = cum[..., :, None] - cum[..., None, :]
        decay = jnp.where(tri, jnp.exp(jnp.where(tri, seg, 0.0)), 0.0)
        dt_t = jnp.moveaxis(dt_, 1, -1)
        cb = jnp.einsum("bign,bjgn->bgij", c_, b_)
        w = cb[:, :, None] * decay * dt_t[..., None, :]
        y = jnp.einsum("bgrij,bjgrp->bigrp", w, x_)
        y = y + jnp.einsum("bign,bgrpn->bigrp", c_, state) * jnp.exp(jnp.moveaxis(cum, -1, 1))[..., None]
        last = cum[..., -1:]
        w_state = jnp.exp(last - cum) * dt_t
        new_state = jnp.exp(last)[..., None] * state + jnp.einsum("bjgn,bgrj,bjgrp->bgrpn", b_, w_state, x_)
        return new_state, y

    state, ys = lax.scan(step, h0, (xq, laq, dtq, bq, cq))
    return jnp.moveaxis(ys, 0, 1).reshape(b, l, h, p), state

def ssd_mixer(hx, hc, w_in, conv_w, conv_b, a_log, dt_bias, d_skip, norm_g, w_out, need_ctx):
    def project(h):
        b, l, _ = h.shape
        z, xbc, dt = jnp.split(h @ w_in, [SSM_D_INNER, SSM_D_INNER + SSM_CONV_DIM], axis=-1)
        xbc = jax.nn.silu(centred_dwconv(xbc, conv_w, conv_b))
        xs, bm, cm = jnp.split(xbc, [SSM_D_INNER, SSM_D_INNER + SSM_GROUPS * SSM_STATE], axis=-1)
        dt = jax.nn.softplus(dt.astype(F32).reshape(b, l, 2, SSM_HEADS) + dt_bias.astype(F32))
        return (z, xs.reshape(b, l, SSM_HEADS, SSM_HEAD_DIM),
                bm.reshape(b, l, SSM_GROUPS, SSM_STATE), cm.reshape(b, l, SSM_GROUPS, SSM_STATE), dt)

    zx, xx, bx, cx, dtx = project(hx)
    zc, xc, bc, cc, dtc = project(hc)
    a = -jnp.exp(a_log.astype(F32))
    dsk = d_skip.astype(F32)[:, None]
    y_lat = dsk * xx.astype(F32)
    y_ctx = dsk * xc.astype(F32)
    bsz = hx.shape[0]
    for direction in range(2):
        rev = direction == 1
        f = (lambda t: jnp.flip(t, axis=1)) if rev else (lambda t: t)
        h0 = jnp.zeros((bsz, SSM_GROUPS, SSM_HEADS // SSM_GROUPS, SSM_HEAD_DIM, SSM_STATE), F32)
        yc_d, hc_final = ssd_scan(f(xc), f(dtc[:, :, direction]), a[direction], f(bc), f(cc), h0)
        yx_d, _ = ssd_scan(f(xx), f(dtx[:, :, direction]), a[direction], f(bx), f(cx), hc_final)
        y_lat = y_lat + f(yx_d)
        y_ctx = y_ctx + f(yc_d)

    def finish(y, z):
        b, l = y.shape[:2]
        y = y.reshape(b, l, SSM_D_INNER).astype(z.dtype)
        return rms_norm(y * jax.nn.silu(z), norm_g) @ w_out

    return finish(y_lat, zx), (finish(y_ctx, zc) if need_ctx else None)

def window_gqa_mixer(hx, hc, w_qkv, q_g, k_g, sinks, w_out, cos, sin, need_ctx):
    grp = WIN_HEADS // WIN_KV_HEADS

    def qkv(h):
        b, l, _ = h.shape
        q, k, v = jnp.split(h @ w_qkv, [WIN_HEADS * HEAD_DIM, (WIN_HEADS + WIN_KV_HEADS) * HEAD_DIM], axis=-1)
        q = rms_norm(q.reshape(b, l, WIN_HEADS, HEAD_DIM), q_g)
        k = rms_norm(k.reshape(b, l, WIN_KV_HEADS, HEAD_DIM), k_g)
        return q, k, v.reshape(b, l, WIN_KV_HEADS, HEAD_DIM)

    qx, kx, vx = qkv(hx)
    qc, kc, vc = qkv(hc)
    qx = apply_rope(qx, cos, sin)
    kx = apply_rope(kx, cos, sin)
    b, s = hx.shape[:2]
    n_ctx = hc.shape[1]
    nb = s // BLOCK
    scale = HEAD_DIM ** -0.5
    sink = sinks.astype(F32).reshape(WIN_KV_HEADS, grp)[None, :, :, None, None]

    kpad = jnp.pad(kx, ((0, 0), (BLOCK, BLOCK), (0, 0), (0, 0)))
    vpad = jnp.pad(vx, ((0, 0), (BLOCK, BLOCK), (0, 0), (0, 0)))
    qblocks = jnp.moveaxis(qx.reshape(b, nb, BLOCK, WIN_KV_HEADS, grp, HEAD_DIM), 1, 0)
    rel = (jnp.arange(3 * BLOCK) - BLOCK)[None, :] - jnp.arange(BLOCK)[:, None]
    in_band = jnp.abs(rel) <= WINDOW

    def block_fn(args):
        q, n = args
        start = n * BLOCK
        k = lax.dynamic_slice_in_dim(kpad, start, 3 * BLOCK, axis=1)
        v = lax.dynamic_slice_in_dim(vpad, start, 3 * BLOCK, axis=1)
        kpos = start - BLOCK + jnp.arange(3 * BLOCK)
        mask = in_band & ((kpos >= 0) & (kpos < s))[None, :]
        s_lat = jnp.einsum("bqkgd,bjkd->bkgqj", q, k).astype(F32) * scale
        s_lat = jnp.where(mask, s_lat, -jnp.inf)
        s_ctx = jnp.einsum("bqkgd,bjkd->bkgqj", q, kc).astype(F32) * scale
        sink_b = jnp.broadcast_to(sink, (b, WIN_KV_HEADS, grp, BLOCK, 1))
        p = jax.nn.softmax(jnp.concatenate([s_lat, s_ctx, sink_b], axis=-1), axis=-1).astype(v.dtype)
        o = jnp.einsum("bkgqj,bjkd->bqkgd", p[..., :3 * BLOCK], v)
        return o + jnp.einsum("bkgqj,bjkd->bqkgd", p[..., 3 * BLOCK:3 * BLOCK + n_ctx], vc)

    o = lax.map(block_fn, (qblocks, jnp.arange(nb)))
    yx = jnp.moveaxis(o, 0, 1).reshape(b, s, WIN_HEADS * HEAD_DIM) @ w_out
    yc = None
    if need_ctx:
        qcb = qc.reshape(b, n_ctx, WIN_KV_HEADS, grp, HEAD_DIM)
        s_cc = jnp.einsum("bqkgd,bjkd->bkgqj", qcb, kc).astype(F32) * scale
        sink_c = jnp.broadcast_to(sink, (b, WIN_KV_HEADS, grp, n_ctx, 1))
        p = jax.nn.softmax(jnp.concatenate([s_cc, sink_c], axis=-1), axis=-1).astype(vc.dtype)
        oc = jnp.einsum("bkgqj,bjkd->bqkgd", p[..., :n_ctx], vc)
        yc = oc.reshape(b, n_ctx, WIN_HEADS * HEAD_DIM) @ w_out
    return yx, yc

def diff_attn_mixer(hx, hc, w_qkv, q_g, k_g, lam, subln_g, w_out, lam_init, cos, sin, need_ctx):
    def qkv(h):
        b, l, _ = h.shape
        q, k, v = jnp.split(h @ w_qkv, [2 * DIFF_HEADS * HEAD_DIM, 4 * DIFF_HEADS * HEAD_DIM], axis=-1)
        q = rms_norm(q.reshape(b, l, 2 * DIFF_HEADS, HEAD_DIM), q_g)
        k = rms_norm(k.reshape(b, l, 2 * DIFF_HEADS, HEAD_DIM), k_g)
        return q, k, v.reshape(b, l, DIFF_HEADS, 2 * HEAD_DIM)

    qx, kx, vx = qkv(hx)
    qc, kc, vc = qkv(hc)
    qx = apply_rope(qx, cos, sin)
    kx = apply_rope(kx, cos, sin)
    lf = lam.astype(F32)
    lam_full = jnp.exp(jnp.sum(lf[0] * lf[1])) - jnp.exp(jnp.sum(lf[2] * lf[3])) + lam_init
    scale = HEAD_DIM ** -0.5

    def attend(q, k, v):
        bq, nq = q.shape[:2]
        logits = jnp.einsum("bqhd,bjhd->bhqj", q, k).astype(F32) * scale
        p = jax.nn.softmax(logits, axis=-1).reshape(bq, DIFF_HEADS, 2, nq, k.shape[1])
        w = (p[:, :, 0] - lam_full * p[:, :, 1]).astype(v.dtype)
        o = jnp.einsum("bhqj,bjhe->bqhe", w, v)
        o = rms_norm(o, subln_g) * (1.0 - lam_init)
        return o.reshape(bq, nq, DIFF_HEADS * 2 * HEAD_DIM)

    b, s = hx.shape[:2]
    nb = s // BLOCK
    k_all = jnp.concatenate([kx, kc], axis=1)
    v_all = jnp.concatenate([vx, vc], axis=1)
    qblocks = jnp.moveaxis(qx.reshape(b, nb, BLOCK, 2 * DIFF_HEADS, HEAD_DIM), 1, 0)
    o = lax.map(lambda q: attend(q, k_all, v_all), qblocks)
    yx = jnp.moveaxis(o, 0, 1).reshape(b, s, D_MODEL) @ w_out
    yc = attend(qc, kc, vc) @ w_out if need_ctx else None
    return yx, yc

def hier_moe(t, w_group, b_group, w_expert, b_expert, w_gate, w_up, w_down):
    n, d = t.shape
    g_prob = jax.nn.softmax((t @ w_group).astype(F32) + b_group.astype(F32), axis=-1)
    g_p, g_sel = lax.top_k(g_prob, 1)
    e_logits = ((t @ w_expert).astype(F32) + b_expert.astype(F32)).reshape(n, MOE_GROUPS, MOE_EXPERTS_PER_GROUP)
    sel_idx = jnp.broadcast_to(g_sel[:, :, None], (n, 1, MOE_EXPERTS_PER_GROUP))
    e_logits = jnp.take_along_axis(e_logits, sel_idx, axis=1)[:, 0]
    e_p, e_sel = lax.top_k(jax.nn.softmax(e_logits, axis=-1), MOE_TOP_K)
    gate = g_p * e_p / jnp.sum(e_p, axis=-1, keepdims=True)
    expert = (g_sel * MOE_EXPERTS_PER_GROUP + e_sel).reshape(-1).astype(jnp.int32)

    n_assign = n * MOE_TOP_K
    a_tok = jnp.repeat(jnp.arange(n, dtype=jnp.int32), MOE_TOP_K)
    a_w = gate.reshape(-1)
    counts = jax.ops.segment_sum(jnp.ones_like(expert), expert, num_segments=MOE_EXPERTS)
    padded = (counts + MOE_BLOCK - 1) // MOE_BLOCK * MOE_BLOCK
    pad_end = jnp.cumsum(padded)
    pad_start = pad_end - padded
    start = jnp.cumsum(counts) - counts
    order = jnp.argsort(expert)
    sorted_exp = expert[order]
    dest = pad_start[sorted_exp] + jnp.arange(n_assign, dtype=jnp.int32) - start[sorted_exp]
    n_blocks = (n_assign + MOE_EXPERTS * (MOE_BLOCK - 1) + MOE_BLOCK - 1) // MOE_BLOCK
    slot_tok = jnp.full((n_blocks * MOE_BLOCK,), n, jnp.int32).at[dest].set(a_tok[order])
    slot_w = jnp.zeros((n_blocks * MOE_BLOCK,), F32).at[dest].set(a_w[order])
    block_starts = jnp.arange(n_blocks, dtype=jnp.int32) * MOE_BLOCK
    block_exp = jnp.minimum(jnp.searchsorted(pad_end, block_starts, side="right"), MOE_EXPERTS - 1)
    t_pad = jnp.concatenate([t, jnp.zeros((1, d), t.dtype)], axis=0)

    def expert_block(args):
        tok, e = args
        xb = t_pad[tok]
        hdn = jax.nn.silu(xb @ w_gate[e]) * (xb @ w_up[e])
        return hdn @ w_down[e]

    ys = lax.map(expert_block, (slot_tok.reshape(n_blocks, MOE_BLOCK), block_exp))
    ys = ys.reshape(-1, d) * slot_w.astype(t.dtype)[:, None]
    return jax.ops.segment_sum(ys, slot_tok, num_segments=n + 1)[:n]

def setup_inputs(seed: int = 0) -> dict:
    key = jax.random.key(seed)
    ks = iter(jax.random.split(key, 48))

    def nrm(shape, scale):
        return jax.random.normal(next(ks), shape, F32) * scale

    def gain(shape):
        return 1.0 + nrm(shape, 0.05)

    D = D_MODEL
    u_a = jax.random.uniform(next(ks), (N_LAYERS_A, 2, SSM_HEADS), F32, minval=1.0, maxval=16.0)
    u_dt = jax.random.uniform(next(ks), (N_LAYERS_A, 2, SSM_HEADS), F32)
    dt0 = jnp.exp(u_dt * (math.log(0.1) - math.log(1e-3)) + math.log(1e-3))
    return {
        "x": nrm((BATCH, SEQ, D), 1.0),
        "c": nrm((BATCH, D), 1.0),
        "ctx": nrm((BATCH, CTX_LEN, D), 1.0),
        "c_ctx": nrm((D,), 1.0),
        "ada_w": nrm((DEPTH, D, 6 * D), 0.5 * D ** -0.5),
        "ada_b": nrm((DEPTH, 6 * D), 0.02),
        "norm_g": gain((DEPTH, 2, D)),
        "ssm_w_in": nrm((N_LAYERS_A, D, SSM_IN_DIM), D ** -0.5),
        "ssm_conv_w": nrm((N_LAYERS_A, SSM_CONV, SSM_CONV_DIM), SSM_CONV ** -0.5),
        "ssm_conv_b": nrm((N_LAYERS_A, SSM_CONV_DIM), 0.02),
        "ssm_a_log": jnp.log(u_a),
        "ssm_dt_bias": dt0 + jnp.log(-jnp.expm1(-dt0)),
        "ssm_d": 1.0 + nrm((N_LAYERS_A, SSM_HEADS), 0.1),
        "ssm_norm_g": gain((N_LAYERS_A, SSM_D_INNER)),
        "ssm_w_out": nrm((N_LAYERS_A, SSM_D_INNER, D), SSM_D_INNER ** -0.5),
        "win_w_qkv": nrm((N_LAYERS_B, D, (WIN_HEADS + 2 * WIN_KV_HEADS) * HEAD_DIM), D ** -0.5),
        "win_q_g": gain((N_LAYERS_B, HEAD_DIM)),
        "win_k_g": gain((N_LAYERS_B, HEAD_DIM)),
        "win_sinks": nrm((N_LAYERS_B, WIN_HEADS), 0.5),
        "win_w_out": nrm((N_LAYERS_B, WIN_HEADS * HEAD_DIM, D), (WIN_HEADS * HEAD_DIM) ** -0.5),
        "diff_w_qkv": nrm((N_LAYERS_C, D, 6 * DIFF_HEADS * HEAD_DIM), D ** -0.5),
        "diff_q_g": gain((N_LAYERS_C, HEAD_DIM)),
        "diff_k_g": gain((N_LAYERS_C, HEAD_DIM)),
        "diff_lam": nrm((N_LAYERS_C, 4, HEAD_DIM), 0.1),
        "diff_subln_g": gain((N_LAYERS_C, 2 * HEAD_DIM)),
        "diff_w_out": nrm((N_LAYERS_C, D, D), D ** -0.5),
        "moe_w_group": nrm((DEPTH, D, MOE_GROUPS), D ** -0.5),
        "moe_b_group": nrm((DEPTH, MOE_GROUPS), 0.01),
        "moe_w_expert": nrm((DEPTH, D, MOE_EXPERTS), D ** -0.5),
        "moe_b_expert": nrm((DEPTH, MOE_EXPERTS), 0.01),
        "moe_w_gate": nrm((DEPTH, MOE_EXPERTS, D, MOE_D_FF), D ** -0.5),
        "moe_w_up": nrm((DEPTH, MOE_EXPERTS, D, MOE_D_FF), D ** -0.5),
        "moe_w_down": nrm((DEPTH, MOE_EXPERTS, MOE_D_FF, D), MOE_D_FF ** -0.5),
    }

def reference(x, c, ctx, c_ctx, ada_w, ada_b, norm_g,
              ssm_w_in, ssm_conv_w, ssm_conv_b, ssm_a_log, ssm_dt_bias, ssm_d, ssm_norm_g, ssm_w_out,
              win_w_qkv, win_q_g, win_k_g, win_sinks, win_w_out,
              diff_w_qkv, diff_q_g, diff_k_g, diff_lam, diff_subln_g, diff_w_out,
              moe_w_group, moe_b_group, moe_w_expert, moe_b_expert, moe_w_gate, moe_w_up, moe_w_down):
    b, s, d = x.shape
    n_ctx = ctx.shape[1]
    cos, sin = axial_rope(s, HEAD_DIM)
    for i in range(DEPTH):
        kind = i % N_MIXERS
        j = i // N_MIXERS
        need_ctx = i < DEPTH - 1
        mx = modulation(c, ada_w[i], ada_b[i])
        mc = modulation(c_ctx, ada_w[i], ada_b[i])
        hx = modulate(rms_norm(x, norm_g[i, 0]), mx[0][:, None], mx[1][:, None])
        hc = modulate(rms_norm(ctx, norm_g[i, 0]), mc[0], mc[1])
        if kind == 0:
            yx, yc = ssd_mixer(hx, hc, ssm_w_in[j], ssm_conv_w[j], ssm_conv_b[j], ssm_a_log[j],
                               ssm_dt_bias[j], ssm_d[j], ssm_norm_g[j], ssm_w_out[j], need_ctx)
        elif kind == 1:
            yx, yc = window_gqa_mixer(hx, hc, win_w_qkv[j], win_q_g[j], win_k_g[j], win_sinks[j],
                                      win_w_out[j], cos, sin, need_ctx)
        else:
            lam_init = 0.8 - 0.6 * math.exp(-0.3 * i)
            yx, yc = diff_attn_mixer(hx, hc, diff_w_qkv[j], diff_q_g[j], diff_k_g[j], diff_lam[j],
                                     diff_subln_g[j], diff_w_out[j], lam_init, cos, sin, need_ctx)
        x = x + mx[2][:, None] * yx
        hx = modulate(rms_norm(x, norm_g[i, 1]), mx[3][:, None], mx[4][:, None])
        if need_ctx:
            ctx = ctx + mc[2] * yc
            hc = modulate(rms_norm(ctx, norm_g[i, 1]), mc[3], mc[4])
            tokens = jnp.concatenate([hx.reshape(-1, d), hc.reshape(-1, d)], axis=0)
        else:
            tokens = hx.reshape(-1, d)
        y = hier_moe(tokens, moe_w_group[i], moe_b_group[i], moe_w_expert[i], moe_b_expert[i],
                     moe_w_gate[i], moe_w_up[i], moe_w_down[i])
        x = x + mx[5][:, None] * y[:b * s].reshape(b, s, d)
        if need_ctx:
            ctx = ctx + mc[5] * y[b * s:].reshape(b, n_ctx, d)
    return x


_drawn_inputs = setup_inputs


def setup_inputs(seed=0):
    import zlib

    import numpy as np

    out = dict(_drawn_inputs(seed))
    spreads = {}
    factors = {'ctx': 11.433,
     'ssm_conv_b': 6.277,
     'ssm_d': 4.723,
     'ssm_norm_g': 3.823,
     'moe_b_group': 42.7,
     'moe_b_expert': 43.791}
    for name, (base, spread) in spreads.items():
        noise = np.random.default_rng([zlib.crc32(name.encode()), seed]).standard_normal(out[name].shape)
        drawn = base * np.exp(spread * noise) if base else spread * noise
        out[name] = jnp.asarray(drawn.astype(out[name].dtype))
    for name, factor in factors.items():
        out[name] = (out[name] * factor).astype(out[name].dtype)
    return out
```

```python
from contextlib import ExitStack

import numpy as np
import concourse.bass as bass
from concourse import mybir

F32 = mybir.dt.float32
F32R = mybir.dt.float32r
I32 = mybir.dt.int32
U32 = mybir.dt.uint32
ALU = mybir.AluOpType
ACT = mybir.ActivationFunctionType
AX_X = mybir.AxisListType.X

P = 128
EPS = 1e-6
NEG = -1.0e30

CHUNKS = [("B", 0), ("C", 0), ("x", 0), ("z", 0), ("z", 1), ("x", 1), ("z", 2), ("z", 3), ("x", 2), ("x", 3)]
NCH = len(CHUNKS)
CONV_AT = {0: 0, 1: 1, 2: 2, 5: 3, 8: 4, 9: 5}
TURN_AT = {0: 0, 2: 1, 5: 2, 8: 3, 9: 4}
NCONV, NTURN = len(CONV_AT), len(TURN_AT)
TURN_BEFORE = {0: -1, 2: 1, 5: 0, 8: 2, 9: 3}
NADA = 8
LOADS = [t for n in range(NADA) for t in (("w", n), ("a", n))] + [("w", 8), ("w", 9)]
RAW = 3
SLOTS = 64


def build(nc, t):
    D = t["x"].shape[2]
    L = t["x"].shape[1]
    LC = t["ctx"].shape[1]
    T = L + LC
    KC = D // P
    TT = L // P
    DI = t["ssm_norm_g"].shape[1]
    IC = DI // P
    HEADS = t["ssm_d"].shape[1]
    CD = t["ssm_conv_w"].shape[2]
    GN = (CD - DI) // 2
    GROUPS = GN // P
    R = HEADS // GROUPS
    GC = IC // GROUPS
    NG, NE, EPG = t["moe_w_group"].shape[2], t["moe_w_expert"].shape[2], t["moe_w_expert"].shape[2] // t["moe_w_group"].shape[2]
    FF = t["moe_w_gate"].shape[3]
    FC = FF // P
    ROWS = 2 * L
    RPAD = ROWS + SLOTS
    ADA1 = 2 * KC
    ADA2 = 4 * KC
    assert L == 256 and LC == 256 and R == 8 and GC == 4 and ADA2 == NADA * GROUPS and TT == 2
    PRE = ADA1 + 1
    assert PRE % RAW == 0 and len(LOADS) % RAW == 0
    OUT0 = PRE + len(LOADS) * GROUPS
    M_OUT = 1 + NCH * GROUPS
    HALF = R // 2
    WC = 3 * P

    w_in = t["ssm_w_in"][0].rearrange("(k p) n -> p k n", p=P)
    ada_w = t["ada_w"][0].rearrange("(k p) n -> p k n", p=P)
    w_out = t["ssm_w_out"][0].rearrange("(k p) n -> k p n", p=P)
    w_gate = t["moe_w_gate"][0].rearrange("e (p c) n -> e p c n", c=KC)
    w_up = t["moe_w_up"][0].rearrange("e (p c) n -> e p c n", c=KC)
    w_down = t["moe_w_down"][0].rearrange("e (f p) n -> e p f n", p=P)
    Z0, X0, B0, C0, DT0 = 0, DI, 2 * DI, 2 * DI + GN, 2 * DI + 2 * GN

    def w_in_at(g, n):
        kind, c = CHUNKS[n]
        return {"z": Z0 + 512 * g + P * c, "x": X0 + 512 * g + P * c, "B": B0 + P * g, "C": C0 + P * g}[kind]

    def conv_col(g, n):
        kind, c = CHUNKS[n]
        return {"x": GC * g + c, "B": IC + g, "C": IC + GROUPS + g}[kind]

    with ExitStack() as ctx:
        def sb(name, shape, dt=F32):
            return ctx.enter_context(nc.sbuf_tensor(name, shape, dt))

        def sem(name):
            return ctx.enter_context(nc.semaphore(name))

        ident = sb("ident", [P, P])
        ones = sb("ones", [P, P])
        tri_up = sb("tri_up", [P, P])
        tri_lo = sb("tri_lo", [P, P])
        strict = sb("strict", [P, P])
        pidx = sb("pidx", [P, 1])
        packs = sb("packs", [P, 3, P])
        adab = packs[:, 0, 0:96]
        g0col, g1col = packs[:, 1, 96:112], packs[:, 1, 112:128]
        ngcol = packs[:, 2, 96:128]
        tapc = sb("tapc", [P, 4, 48])
        cvec = sb("cvec", [P, KC, 2])
        cth = sb("cth", [P, KC, 2])
        adac = sb("adac", [P, 2 * KC, 2])
        acol = sb("acol", [P, KC, 2])
        ada2 = sb("ada2", [P, ADA2])
        dcol = sb("dcol", [P, IC])
        dtb = sb("dtb", [P, 1])
        alog = sb("alog", [P, 1])
        arate = sb("arate", [P, 1])
        tot = sb("tot", [P, 1])
        ssq = sb("ssq", [P, 8])
        rms = sb("rms", [P, 8])
        rstd = sb("rstd", [P, 8])
        tokm = sb("tokm", [P, 6, 2, HEADS])
        tokg = sb("tokg", [P, 6, 2, R])

        KB = 1024
        base = (nc.sbuf_base + 63) // 64 * 64
        ARENA = 197 * KB
        arena = ctx.enter_context(nc.sbuf_tensor("arena", [P, (ARENA + 64) // 4], F32))

        def at(name, kb, shape, dt=F32):
            size = int(np.prod(shape[1:])) * 4
            assert kb * KB + size <= ARENA, name
            return nc.alloc_sbuf_tensor_at(name, shape, dt, offset=base + int(kb * KB))

        hTh = at("hTh", 0, [P, KC, T], F32R)
        hTl = at("hTl", 32, [P, KC, T], F32R)
        raw = at("raw", 64, [P, RAW, D])
        whi = at("whi", 88, [P, 2, D], F32R)
        wlo = at("wlo", 104, [P, 2, D], F32R)
        xtok = at("xtok", 120, [P, 4, 512])
        xdtf = at("xdtf", 128, [P, TT, 512])
        xwf = at("xwf", 132, [P, TT, 512])
        bc = at("bc", 136, [P, R, L])
        ce = at("ce", 144, [P, R, L])
        wts = at("wts", 152, [P, R, WC])
        zs = at("zs", 164, [P, GC, L])
        dx = at("dx", 168, [P, GC, L])
        st = at("st", 172, [P, 2, 512])
        bT = at("bT", 176, [P, L])
        cT = at("cT", 177, [P, L])
        cT2 = at("cT2", 178, [P, L])
        btok = at("btok", 179, [P, TT, P])
        cv = at("cv", 180, [P, 2, T])
        th = at("th", 184, [P, 2, T])
        slx = at("slx", 188, [P, 2, T])
        cbm = at("cbm", 192, [P, 2, WC])
        ybuf = at("ybuf", 195, [P, 2, L])
        xrows = at("xrows", 120, [P, 4, D])
        xnT = at("xnT", 152, [P, KC, T])
        prow = at("prow", 184, [P, 3, P])
        sqr0 = at("sqr0", 186, [P, D])
        dtw = at("dtw", 120, [P, 8, T])
        yraw = at("yraw", 0, [P, IC, L])
        yh = at("yh", 32, [P, IC, L], F32R)
        yl = at("yl", 120, [P, IC, L], F32R)
        ysq = at("ysq", 152, [P, 2, L])
        a2row = at("a2row", 154, [ADA2, P])
        a2c = at("a2c", 156, [P, ADA2])
        gate_b = at("gate_b", 164, [P, D])
        scale_b = at("scale_b", 172, [P, D])
        shift_b = at("shift_b", 180, [P, D])
        x1 = at("x1", 0, [P, TT, D])
        h2 = at("h2", 16, [P, TT, D])
        sqr1 = at("sqr1", 120, [P, D])
        h2T = at("h2T", 32, [P, KC, L])
        rw = at("rw", 188, [P, KC, NG + NE])
        rbias = at("rbias", 190.5, [P, NG + NE])
        iota_r = at("iota_r", 194, [P, RPAD])
        iota_e = at("iota_e", 51, [P, NE])
        rt = at("rt", 48, [P, TT, 11, NE])
        pick = at("pick", 186, [P, TT, 3, NE])
        rs = at("rs", 184, [P, 12, NE])
        ridx = at("ridx", 187, [P, TT, 2, 8], U32)
        onehot = at("onehot", 32, [P, TT, ROWS])
        wonehot = at("wonehot", 36, [P, TT, ROWS])
        oh_tmp = at("oh_tmp", 40, [P, TT, ROWS])
        outT = at("outT", 16, [P, KC, RPAD])
        xgT = at("xgT", 52, [P, KC, RPAD])
        wg = at("wg", 88, [P, KC, FF])
        wu = at("wu", 120, [P, KC, FF])
        wd = at("wd", 152, [P, FC, D])
        gT = at("gT", 184, [P, ROWS // P, L])
        itab = at("itab", 188, [1, 3 * P], I32)
        hdn = at("hdn", 190, [P, FC, SLOTS])
        gtanh = at("gtanh", 191, [P, FC, SLOTS])
        gsil = at("gsil", 192, [P, FC, SLOTS])
        xe = at("xe", 193, [P, KC, SLOTS])
        ys = at("ys", 88, [P, ROWS // P, D])
        gate5_b = at("gate5_b", 120, [P, D])
        ctmp = at("ctmp", 128, [P, 2, 512])
        fin = at("fin", 132, [P, 2, 512])

        banks = [ctx.enter_context(nc.psum_tensor(f"bank{i}", [P, 512], F32)) for i in range(8)]
        TURN, CBK, STK = banks[3], banks[4], [banks[5], banks[4]]
        ADAK = banks[2]

        cum_d = nc.dram_tensor("cum_d", (P, L), F32, kind="Internal").ap()
        y_d = nc.dram_tensor("y_d", (DI, L), F32, kind="Internal").ap()
        mod_d = nc.dram_tensor("mod_d", (ADA2, P), F32, kind="Internal").ap()

        s_pack = sem("s_pack")
        s_x = sem("s_x")
        s_const = sem("s_const")
        s_raw = [sem(f"s_raw{i}") for i in range(RAW)]
        s_ptr = sem("s_ptr")
        s_pk = sem("s_pk")
        s_cth = sem("s_cth")
        s_cvec = sem("s_cvec")
        s_ssq = sem("s_ssq")
        s_mean = sem("s_mean")
        s_rms = sem("s_rms")
        s_rstd = sem("s_rstd")
        s_xn = sem("s_xn")
        s_xt = sem("s_xt")
        s_xte = sem("s_xte")
        s_ada = sem("s_ada")
        s_bT = sem("s_bT")
        s_strict = sem("s_strict")
        s_h = sem("s_h")
        s_hh = sem("s_hh")
        s_hl = sem("s_hl")
        s_hi = sem("s_hi")
        s_lo = sem("s_lo")
        s_win = sem("s_win")
        s_drain = sem("s_drain")
        s_cvA = sem("s_cvA")
        s_cvB = sem("s_cvB")
        s_th = sem("s_th")
        s_prod = sem("s_prod")
        s_T = sem("s_T")
        s_Tev = sem("s_Tev")
        s_dx = sem("s_dx")
        s_dtx = sem("s_dtx")
        s_dabs = sem("s_dabs")
        s_dexp = sem("s_dexp")
        s_du = sem("s_du")
        s_dln = sem("s_dln")
        s_cumr = sem("s_cumr")
        s_dw = sem("s_dw")
        s_dec = sem("s_dec")
        s_dtT = sem("s_dtT")
        s_tokm = sem("s_tokm")
        s_bc = sem("s_bc")
        s_cb = sem("s_cb")
        s_cbm = sem("s_cbm")
        s_tg = sem("s_tg")
        s_ct2 = sem("s_ct2")
        s_seg = sem("s_seg")
        s_expw = sem("s_expw")
        s_ebc = sem("s_ebc")
        s_wts = sem("s_wts")
        s_ce = sem("s_ce")
        s_xd = sem("s_xd")
        s_st = sem("s_st")
        s_stev = sem("s_stev")
        s_y = sem("s_y")
        s_fin1 = sem("s_fin1")
        s_fin2 = sem("s_fin2")
        s_yst = [sem(f"s_yst{i}") for i in range(2)]
        s_adaev = sem("s_adaev")
        s_yld = [sem(f"s_yld{i}") for i in range(GROUPS)]
        s_ysq = sem("s_ysq")
        s_yss = sem("s_yss")
        s_yh = sem("s_yh")
        s_yl = sem("s_yl")
        s_a2 = sem("s_a2")
        s_a2T = sem("s_a2T")
        s_a2r = sem("s_a2r")
        s_mod = sem("s_mod")
        s_modb = sem("s_modb")
        s_xres = sem("s_xres")
        s_wo = sem("s_wo")
        s_x1a = sem("s_x1a")
        s_x1 = sem("s_x1")
        s_h2a = sem("s_h2a")
        s_h2 = sem("s_h2")
        s_h2t = sem("s_h2t")
        s_h2tA = sem("s_h2tA")
        s_h2tV = sem("s_h2tV")
        s_logit = sem("s_logit")
        s_gmax = sem("s_gmax")
        s_gexp = sem("s_gexp")
        s_ediff = sem("s_ediff")
        s_eexp = sem("s_eexp")
        s_pick = sem("s_pick")
        s_rank = sem("s_rank")
        s_tabc = sem("s_tabc")
        s_tabr = sem("s_tabr")
        s_place = sem("s_place")
        s_gTp = sem("s_gTp")
        s_gTv = sem("s_gTv")
        s_rwl = sem("s_rwl")
        s_iota = sem("s_iota")
        s_xg = sem("s_xg")
        s_xgA = sem("s_xgA")
        s_xgV = sem("s_xgV")
        s_tab = sem("s_tab")
        s_v = sem("s_v")
        s_pad = sem("s_pad")
        s_ld = [sem(f"s_ld{i}") for i in range(6)]
        s_use = [sem(f"s_use{i}") for i in range(6)]
        s_xe = sem("s_xe")
        s_gt = sem("s_gt")
        s_gs = sem("s_gs")
        s_hd = sem("s_hd")
        GATE, UP, DOWN = 1, 3, 5
        s_oA = sem("s_oA")
        s_oV = sem("s_oV")
        s_g5 = sem("s_g5")
        s_fT = sem("s_fT")
        s_fTe = sem("s_fTe")
        s_fy = sem("s_fy")
        s_f1 = sem("s_f1")
        s_f2 = sem("s_f2")
        s_out = [sem(f"s_out{i}") for i in range(2)]

        block = ctx.enter_context(nc.Block())

        def w_view(ring, slot):
            return ring[:, slot, :].rearrange("p (k n) -> p k n", k=KC)

        def raw_of(pos):
            return pos % RAW

        def raw_count(idx3, pos):
            return 16 * (idx3 + pos // RAW + 1)

        POS = {x: i for i, x in enumerate(LOADS)}

        def group_raw(g):
            return PRE // RAW + (len(LOADS) // RAW) * g

        @block.sync
        def _(sp):
            ab = t["ada_b"][0].rearrange("(a b) -> a b", b=P)
            cw = t["ssm_conv_w"][0].rearrange("s (a b) -> (s a) b", b=P)
            col = lambda v: v.rearrange("(a b) -> a b", b=P)
            sp.dma_start(prow[0:96, 0, :], ab).then_inc(s_pack, 16)
            sp.dma_start(prow[96:112, 0, :], col(t["c"][0])).then_inc(s_pack, 16)
            sp.dma_start(prow[112:128, 0, :], col(t["c_ctx"])).then_inc(s_pack, 16)
            sp.dma_start(xrows[:, 0:2, :], t["x"][0].rearrange("(t p) d -> p t d", p=P)).then_inc(s_x, 16)
            sp.dma_start(xrows[:, 2:4, :], t["ctx"][0].rearrange("(t p) d -> p t d", p=P)).then_inc(s_x, 16)
            sp.dma_start(prow[0:96, 1, :], cw[0:96, :]).then_inc(s_pack, 16)
            sp.dma_start(prow[96:112, 1, :], col(t["norm_g"][0, 0])).then_inc(s_pack, 16)
            sp.dma_start(prow[112:128, 1, :], col(t["norm_g"][0, 1])).then_inc(s_pack, 16)
            sp.dma_start(prow[0:48, 2, :], cw[96:144, :]).then_inc(s_pack, 16)
            sp.dma_start(prow[48:96, 2, :], col(t["ssm_conv_b"][0])).then_inc(s_pack, 16)
            sp.dma_start(prow[96:128, 2, :], col(t["ssm_norm_g"][0])).then_inc(s_pack, 16)
            sp.dma_start(dtb[:, :], t["ssm_dt_bias"][0].rearrange("a (h o) -> (a h) o", o=1)).then_inc(s_pack, 16)
            sp.dma_start(alog[:, :], t["ssm_a_log"][0].rearrange("a (h o) -> (a h) o", o=1)).then_inc(s_pack, 16)
            dd = t["ssm_d"][0].rearrange("(c two) -> two c", two=2)
            with nc.allow_non_contiguous_dma(reason="64 values"):
                sp.dma_start(dcol[0:64, :], dd[0].partition_broadcast(64)).then_inc(s_pack, 16)
                sp.dma_start(dcol[64:128, :], dd[1].partition_broadcast(64)).then_inc(s_pack, 16)
            for a in range(ADA1):
                if a >= RAW:
                    sp.wait_ge(s_ada, a - RAW + 1)
                sp.dma_start(w_view(raw, a % RAW), ada_w[:, :, P * a:P * a + P]).then_inc(s_raw[a % RAW], 16)
            sp.wait_ge(s_ada, ADA1 - RAW + 1)
            sp.dma_start(w_view(raw, ADA1 % RAW), w_in[:, :, DT0:DT0 + P]).then_inc(s_raw[ADA1 % RAW], 16)

            def slot_free(g, pos, first):
                if pos >= RAW:
                    (kind, n), bg = LOADS[pos - RAW], g
                elif not first:
                    (kind, n), bg = LOADS[pos - RAW + len(LOADS)], g - 1
                elif pos < RAW - 1:
                    sp.wait_ge(s_ada, ADA1 - (RAW - 1) + pos + 1)
                    return
                else:
                    sp.wait_ge(s_lo, 1)
                    return
                if kind == "w":
                    sp.wait_ge(s_lo, NCH * bg + (n + 2))
                else:
                    sp.wait_ge(s_ada, NADA * bg + (ADA1 + n + 1))

            def group_loads(g, first=False):
                for pos, (kind, n) in enumerate(LOADS):
                    slot_free(g, pos, first)
                    if kind == "w" and CHUNKS[n] == ("z", 0):
                        src = w_in[:, :, bass.ds(g * 256 + g * 256, P)]
                    elif kind == "w":
                        src = w_in[:, :, bass.ds(w_in_at(g, n), P)]
                    else:
                        src = ada_w[:, :, bass.ds(P * NADA * g + P * (ADA1 + n), P)]
                    sp.dma_start(w_view(raw, raw_of(pos)), src).then_inc(s_raw[raw_of(pos)], 16)

            group_loads(0, first=True)
            with sp.Fori(1, GROUPS) as g:
                group_loads(g)

            def y_load(g):
                for i in range(2):
                    sp.wait_ge(s_yst[i], 16 * 2 * (g + 1) + 16)
                sp.dma_start(yraw[:, GC * g:GC * g + GC, :],
                             y_d[512 * g:512 * g + 512, :].rearrange("(c p) t -> p c t", p=P)).then_inc(s_yld[g], 16)

            sp.wait_ge(s_win, M_OUT)
            for g in range(GROUPS - 1):
                y_load(g)
            for k in range(IC):
                if k < RAW:
                    bk, bn = LOADS[len(LOADS) - RAW + k]
                    if bk == "w":
                        sp.wait_ge(s_lo, NCH * (GROUPS - 1) + bn + 2)
                    else:
                        sp.wait_ge(s_ada, ADA1 + NADA * (GROUPS - 1) + bn + 1)
                else:
                    sp.wait_ge(s_lo, M_OUT + k - RAW + 1)
                sp.dma_start(raw[:, (OUT0 + k) % RAW, :], w_out[k]).then_inc(s_raw[(OUT0 + k) % RAW], 16)
                if k == 2:
                    y_load(GROUPS - 1)
                    sp.wait_ge(s_fin2, IC)
                    sp.dma_start(rw[:, :, 0:NG], t["moe_w_group"][0].rearrange("(k p) n -> p k n", p=P)).then_inc(s_rwl, 16)
                    sp.dma_start(rw[:, :, NG:NG + NE], t["moe_w_expert"][0].rearrange("(k p) n -> p k n", p=P)).then_inc(s_rwl, 16)
                    sp.dma_start(rbias[:, 0:NG], t["moe_b_group"][0].partition_broadcast(P)).then_inc(s_rwl, 16)
                    sp.dma_start(rbias[:, NG:NG + NE], t["moe_b_expert"][0].partition_broadcast(P)).then_inc(s_rwl, 16)
            sp.wait_ge(s_yl, IC)
            sp.dma_start(x1[:, :, :], t["x"][0].rearrange("(t p) d -> p t d", p=P)).then_inc(s_xres, 16)

            sp.wait_ge(s_tab, 1)
            nblk = sp.value_load(itab[0:1, 2 * P:2 * P + 1], min_val=1, max_val=P)
            with sp.Fori(0, nblk) as b:
                e = sp.value_load(itab[0:1, bass.ds(b, 1)], min_val=0, max_val=NE - 1)
                for u, (dst, src, n) in enumerate(((wg, w_gate, KC), (wu, w_up, KC), (wd, w_down, FC))):
                    for hf in range(2):
                        i = 2 * u + hf
                        sp.wait_ge(s_use[i], b + 1)
                        sp.dma_start(dst[:, hf * n // 2:(hf + 1) * n // 2, :],
                                     src[bass.ds(e, 1), :, hf * n // 2:(hf + 1) * n // 2, :].rearrange("o p c n -> (o p) c n")
                                     ).then_inc(s_ld[i], 16)
            for i in range(6):
                sp.wait_ge(s_use[i], nblk + 1)
            sp.dma_start(gate5_b[:, :], mod_d[3 * KC:4 * KC, :].rearrange("a b -> (a b)").partition_broadcast(P)).then_inc(s_g5, 16)
            for q in range(2 * TT * 2):
                tt, nb = q // 4, q % 4
                sp.wait_ge(s_f2, q + 1)
                sp.dma_start(t["out"][0, tt * P:(tt + 1) * P, nb * 512:nb * 512 + 512], fin[:, q % 2, :]).then_inc(s_out[q % 2], 16)
            for i in range(2):
                sp.wait_ge(s_out[i], 16 * TT * 2)

        @block.gpsimd
        def _(pool):
            pool.memset(ident[:, :], 0.0).then_inc(s_const, 1)
            pool.memset(ones[:, :], 1.0).then_inc(s_const, 1)
            pool.iota(pidx[:, :], pattern=[[0, 1]], base=0, channel_multiplier=1,
                      allow_small_or_imprecise_dtypes=True).then_inc(s_const, 1)
            pool.wait_ge(s_const, 3)
            pool.affine_select(out=ident[:, :], in_=ident[:, :], compare_op=ALU.not_equal, fill=1.0, base=0,
                               pattern=[[-1, P]], channel_multiplier=1).then_inc(s_const, 1)
            pool.affine_select(out=tri_up[:, :], in_=ones[:, :], compare_op=ALU.is_ge, fill=0.0, base=0,
                               pattern=[[1, P]], channel_multiplier=-1).then_inc(s_const, 1)
            pool.affine_select(out=tri_lo[:, :], in_=ones[:, :], compare_op=ALU.is_ge, fill=0.0, base=0,
                               pattern=[[-1, P]], channel_multiplier=1).then_inc(s_const, 1)
            pool.affine_select(out=strict[:, :], in_=ones[:, :], compare_op=ALU.is_gt, fill=0.0, base=0,
                               pattern=[[1, P]], channel_multiplier=-1).then_inc(s_strict, 1)
            pool.wait_ge(s_cumr, 1)
            for i in range(2):
                rows = slice(HEADS * i, HEADS * (i + 1))
                pool.dma_start(cum_d[rows, :], dtw[rows, 6, 0:L]).then_inc(s_yst[i], 16)
            for i in range(2):
                pool.wait_ge(s_yst[i], 16)

            def load_bc(s, hf):
                for d in range(2):
                    src = cum_d[bass.ds(R * s + (d * HEADS + HALF * hf), HALF), :].rearrange("a b -> (a b)").partition_broadcast(P)
                    dst = bc[:, d * HALF:(d + 1) * HALF, :].rearrange("p a b -> p (a b)")
                    pool.dma_start(dst, src).then_inc(s_bc, 16)

            def group_io(s):
                pool.wait_ge(s_seg, 2 * s + 1)
                pool.wait_ge(s_ebc, 2 * s + 1)
                load_bc(s, 1)
                for c in range(GC):
                    pool.wait_ge(s_fin2, GC * s + c + 1)
                    pool.dma_start(y_d[bass.ds(512 * s + P * c, P), :], ybuf[:, c % 2, :]).then_inc(s_yst[c % 2], 16)

            load_bc(0, 0)
            with pool.Fori(0, GROUPS - 1) as s:
                group_io(s)
                pool.wait_ge(s_seg, 2 * s + 2)
                pool.wait_ge(s_ebc, 2 * s + 2)
                load_bc(s + 1, 0)
            group_io(GROUPS - 1)

            pool.wait_ge(s_a2r, 1)
            pool.dma_start(mod_d[:, :], a2row[:, :]).then_inc(s_mod, 16)
            pool.wait_ge(s_mod, 16)
            pool.wait_ge(s_fin2, IC)
            for i, dst in enumerate((gate_b, shift_b, scale_b)):
                pool.dma_start(dst[:, :], mod_d[KC * i:KC * i + KC, :].rearrange("a b -> (a b)").partition_broadcast(P)).then_inc(s_modb, 16)
            pool.wait_ge(s_wo, IC)
            pool.iota(iota_r[:, :], pattern=[[1, RPAD]], base=0, channel_multiplier=0,
                      allow_small_or_imprecise_dtypes=True).then_inc(s_iota, 1)
            pool.iota(iota_e[:, :], pattern=[[1, NE]], base=0, channel_multiplier=0,
                      allow_small_or_imprecise_dtypes=True).then_inc(s_iota, 1)
            pool.memset(xgT[:, :, ROWS:RPAD], 0.0).then_inc(s_pad, 1)

        @block.scalar
        def _(act):
            act.wait_ge(s_pk, 1)
            act.activation(cth[:, :, :], cvec[:, :, :], ACT.Tanh).then_inc(s_cth, 1)
            act.wait_ge(s_x, 32)
            for tt in range(4):
                if tt > 0:
                    act.wait_ge(s_ssq, tt)
                act.activation(sqr0[:, :], xrows[:, tt, :], ACT.Square, accum_out=ssq[:, tt:tt + 1]).then_inc(s_ssq, 1)
            act.wait_ge(s_mean, 1)
            act.activation(rms[:, 0:4], ssq[:, 4:8], ACT.Sqrt).then_inc(s_rms, 1)
            act.wait_ge(s_rstd, 1)
            for tt in range(4):
                act.activation(xrows[:, tt, :], xrows[:, tt, :], ACT.Copy, scale=rstd[:, tt:tt + 1]).then_inc(s_xn, 1)
            for k in range(KC):
                act.wait_ge(s_h, 2 * k + 2)
                act.activation(hTh[:, k, :], xnT[:, k, :], ACT.Copy).then_inc(s_hh, 1)

            def conv_hi(g, n):
                m = NCH * g + (n + 1)
                pos = POS[("w", n)]
                act.wait_ge(s_raw[raw_of(pos)], raw_count(group_raw(g), pos))
                if not (isinstance(g, int) and g == 0 and n == 0):
                    act.wait_ge(s_win, m - 1)
                act.activation(whi[:, (n + 1) % 2, :], raw[:, raw_of(pos), :], ACT.Copy).then_inc(s_hi, 1)

            act.wait_ge(s_raw[ADA1 % RAW], 16 * (ADA1 // RAW + 1))
            act.activation(whi[:, 0, :], raw[:, ADA1 % RAW, :], ACT.Copy).then_inc(s_hi, 1)
            conv_hi(0, 0)
            act.wait_ge(s_dtx, 1)
            act.activation(dtw[:, 1, :], dtw[:, 0, :], ACT.Abs).then_inc(s_dabs, 1)
            act.wait_ge(s_dabs, 1)
            act.activation(dtw[:, 1, :], dtw[:, 1, :], ACT.Exp, scale=-1.0).then_inc(s_dexp, 1)
            act.wait_ge(s_pack, 16 * 13)
            act.activation(arate[:, :], alog[:, :], ACT.Exp).then_inc(s_dexp, 1)
            act.wait_ge(s_du, 1)
            act.activation(dtw[:, 3, :], dtw[:, 2, :], ACT.Ln).then_inc(s_dln, 1)
            act.wait_ge(s_cumr, 1)
            act.activation(dtw[:, 7, 0:LC], dtw[:, 6, L:T], ACT.Exp, scale=-1.0, bias=tot[:, 0:1]).then_inc(s_dw, 1)

            def tanh_of(g, n):
                w = T if CHUNKS[n][0] in "Bx" else L
                act.wait_ge(s_drain, NCH * g + (n + 1))
                act.activation(th[:, n % 2, 0:w], cv[:, n % 2, 0:w], ACT.Tanh).then_inc(s_th, 1)

            def turn_store(g, n):
                i = TURN_AT[n]
                act.wait_ge(s_T, NTURN * g + (i + 1))
                if n == 0:
                    act.activation(btok[:, :, :], TURN[:, 0:2 * P].rearrange("p (t n) -> p t n", t=2), ACT.Copy).then_inc(s_Tev, 1)
                else:
                    c = CHUNKS[n][1]
                    act.activation(xtok[:, :, P * c:P * c + P], TURN[:, :].rearrange("p (t n) -> p t n", t=4), ACT.Copy).then_inc(s_Tev, 1)

            def decays(s, hf):
                i = 2 * s + (hf + 1)
                act.wait_ge(s_seg, i)
                act.activation(wts[:, :, :], wts[:, :, :], ACT.Exp).then_inc(s_expw, 1)
                act.wait_ge(s_bc, 32 * i)
                if hf == 1:
                    act.wait_ge(s_y, GC * s + 2)
                act.activation(ce[:, :, :], bc[:, :, :], ACT.Exp).then_inc(s_ebc, 1)

            def steps(g, w, ssd):
                s = g - 1
                for n in range(NCH):
                    if w and n + 1 < NCH:
                        conv_hi(g, n + 1)
                    if w and n + 1 == NCH:
                        if not (isinstance(g, int) and g == GROUPS - 1):
                            conv_hi(g + 1, 0)
                    if ssd and n in (0, 4):
                        decays(s, n // 4)
                    if n > 0 and w:
                        tanh_of(g, n - 1)
                    if n == 0 and ssd:
                        tanh_of(s, NCH - 1)
                    if w and n in CONV_AT:
                        width = T if CHUNKS[n][0] in "Bx" else L
                        act.wait_ge(s_win, NCH * g + (n + 2))
                        if n >= 2:
                            act.wait_ge(s_prod, NCH * g + (n - 1))
                        elif ssd:
                            act.wait_ge(s_prod, NCH * g + (n - 1))
                        col = conv_col(g, n)
                        act.activation(cv[:, n % 2, 0:width], banks[(n + 1) % 2][:, 0:width], ACT.Identity,
                                       scale=tapc[:, 1, bass.ds(col, 1)], bias=tapc[:, 3, bass.ds(col, 1)]).then_inc(s_cvA, 1)
                    if ssd and n == 0:
                        turn_store(s, 8)
                    if ssd and n == 1:
                        turn_store(s, 9)
                    if ssd and n == 2:
                        act.wait_ge(s_st, s + 1)
                        act.activation(st[:, 0, :], STK[0][:, :], ACT.Copy)
                        act.activation(st[:, 1, :], STK[1][:, :], ACT.Copy).then_inc(s_stev, 1)
                    if w and n in (2, 4, 7):
                        turn_store(g, {2: 0, 4: 2, 7: 5}[n])

            steps(0, True, False)
            with act.Fori(1, GROUPS - 1) as g:
                steps(g, True, True)
            steps(GROUPS - 1, True, True)
            steps(GROUPS, False, True)

            act.wait_ge(s_y, IC)
            for k in range(IC):
                g = k // GC
                if k % GC == 0:
                    act.wait_ge(s_yld[g], 16)
                if k >= 2:
                    act.wait_ge(s_yss, k - 1)
                act.activation(ysq[:, k % 2, :], yraw[:, k, :], ACT.Square).then_inc(s_ysq, 1)
            act.wait_ge(s_mean, 2)
            act.activation(rms[:, 4:6], ssq[:, 0:2], ACT.Sqrt).then_inc(s_rms, 1)
            for k in range(IC):
                act.activation(yh[:, k, :], yraw[:, k, :], ACT.Copy, scale=ngcol[:, k:k + 1]).then_inc(s_yh, 1)
                m = M_OUT + k
                act.wait_ge(s_raw[(OUT0 + k) % RAW], 16 * ((OUT0 + k) // RAW + 1))
                if k >= 2:
                    act.wait_ge(s_wo, k - 1)
                act.activation(whi[:, m % 2, :], raw[:, (OUT0 + k) % RAW, :], ACT.Copy).then_inc(s_hi, 1)
            for tt in range(TT):
                act.wait_ge(s_x1, 4 * (tt + 1))
                act.wait_ge(s_ssq, 4 + tt)
                act.activation(sqr1[:, :], x1[:, tt, :], ACT.Square, accum_out=ssq[:, 2 + tt:3 + tt]).then_inc(s_ssq, 1)
            act.wait_ge(s_mean, 3)
            act.activation(rms[:, 6:8], ssq[:, 4:6], ACT.Sqrt).then_inc(s_rms, 1)
            for k in range(1, KC, 2):
                act.wait_ge(s_h2t, k + 1)
                act.activation(h2T[:, k, :], banks[k % 2][:, 0:L], ACT.Copy).then_inc(s_h2tA, 1)
            for tt in range(TT):
                act.wait_ge(s_gmax, tt + 1)
                act.activation(rt[:, tt, 3, 0:NG], rt[:, tt, 0, 0:NG], ACT.Exp, bias=rt[:, tt, 2, 8:9],
                               accum_out=rt[:, tt, 3, 8:9]).then_inc(s_gexp, 1)
            for tt in range(TT):
                act.wait_ge(s_ediff, tt + 1)
                act.activation(rt[:, tt, 3, 10:11], rt[:, tt, 3, 9:10], ACT.Exp).then_inc(s_eexp, 1)
            for k in range(1, KC, 2):
                act.wait_ge(s_xg, k + 1)
                act.activation(xgT[:, k, 0:ROWS], banks[4 + k % 4][:, :], ACT.Copy).then_inc(s_xgA, 1)

            act.wait_ge(s_tab, 1)
            nblk = act.value_load(itab[0:1, 2 * P:2 * P + 1], min_val=1, max_val=P)
            with act.Fori(0, nblk) as b:
                start = act.value_load(itab[0:1, bass.ds(b + P, 1)], min_val=0, max_val=ROWS)
                act.wait_ge(s_use[GATE], b + 2)
                act.activation(gtanh[:, :, :], banks[0][:, 0:FC * SLOTS].rearrange("p (f n) -> p f n", f=FC), ACT.Tanh, scale=0.5).then_inc(s_gt, 1)
                act.wait_ge(s_use[DOWN], b + 2)
                act.activation(outT[:, 0:KC // 2, bass.ds(start, SLOTS)],
                               banks[2][:, :].rearrange("p (c n) -> p c n", c=KC // 2), ACT.Copy).then_inc(s_oA, 1)
            act.wait_ge(s_use[DOWN], nblk + 1)
            for q in range(ROWS // P * 4):
                act.wait_ge(s_fT, q + 1)
                act.activation(ys[:, q // 4, (q % 4) * 512:(q % 4) * 512 + 512], banks[q % 2][:, :], ACT.Copy).then_inc(s_fTe, 1)


        @block.vector
        def _(dve):
            chained = [0]

            def ch(ins):
                chained[0] += 1
                ins.then_inc(s_v, 1)
                dve.wait_ge(s_v, chained[0])

            dve.wait_ge(s_ptr, 1)
            ch(dve.tensor_copy(packs[:, :, :].rearrange("p a b -> p (a b)"), banks[3][:, 0:3 * P]))
            dve.tensor_scalar(tapc[:, 0:2, :], packs[:, 1, 0:96].rearrange("p (a b) -> p a b", a=2), 0.5, None, ALU.mult)
            dve.tensor_scalar(tapc[:, 2:4, :], packs[:, 2, 0:96].rearrange("p (a b) -> p a b", a=2), 0.5, None, ALU.mult)
            dve.tensor_scalar(cvec[:, :, :], packs[:, 0, 96:128].rearrange("p (s k) -> p k s", s=2), 0.5, None,
                              ALU.mult).then_inc(s_pk, 1)
            dve.wait_ge(s_cth, 1)
            dve.scalar_tensor_tensor(cvec[:, :, :], cth[:, :, :], 1.0, cvec[:, :, :], ALU.add, ALU.mult).then_inc(s_cvec, 1)
            dve.wait_ge(s_ssq, 4)
            dve.tensor_scalar(ssq[:, 4:8], ssq[:, 0:4], 1.0 / D, EPS, ALU.mult, ALU.add).then_inc(s_mean, 1)
            dve.wait_ge(s_rms, 1)
            dve.reciprocal(rstd[:, 0:4], rms[:, 0:4]).then_inc(s_rstd, 1)
            for k in range(KC):
                dve.wait_ge(s_xt, k + 1)
                dve.tensor_copy(xnT[:, k, :], banks[k % 2][:, :]).then_inc(s_xte, 1)
            dve.wait_ge(s_ada, ADA1)
            ch(dve.tensor_tensor(adac[:, :, :], ADAK[:, 0:2 * ADA1].rearrange("p (a s) -> p a s", s=2),
                                 adab[:, 0:ADA1].unsqueeze(2).broadcast_to([P, ADA1, 2]), ALU.add))
            ch(dve.scalar_tensor_tensor(acol[:, :, :], adac[:, KC:2 * KC, :], 1.0,
                                        g0col.unsqueeze(2).broadcast_to([P, KC, 2]), ALU.add, ALU.mult))
            dve.wait_ge(s_xte, KC)
            for k in range(KC):
                for q in range(2):
                    dve.tensor_scalar(xnT[:, k, q * L:(q + 1) * L], xnT[:, k, q * L:(q + 1) * L], acol[:, k, q:q + 1],
                                      adac[:, k, q:q + 1], ALU.mult, ALU.add).then_inc(s_h, 1)
                if k > 0:
                    dve.wait_ge(s_hh, k)
                    dve.tensor_tensor(hTl[:, k - 1, :], xnT[:, k - 1, :], hTh[:, k - 1, :].bitcast(F32), ALU.subtract).then_inc(s_hl, 1)
            dve.wait_ge(s_hh, KC)
            dve.tensor_tensor(hTl[:, KC - 1, :], xnT[:, KC - 1, :], hTh[:, KC - 1, :].bitcast(F32), ALU.subtract).then_inc(s_hl, 1)

            def lo(m, slot, raw_tile, free=True):
                dve.wait_ge(s_hi, m + 1)
                if free:
                    dve.wait_ge(s_win, m - 1)
                dve.tensor_tensor(wlo[:, slot, :], raw_tile, whi[:, slot, :].bitcast(F32), ALU.subtract).then_inc(s_lo, 1)

            def conv_lo(g, n):
                lo(NCH * g + (n + 1), (n + 1) % 2, raw[:, raw_of(POS[("w", n)]), :],
                   free=not (isinstance(g, int) and g == 0 and n == 0))

            lo(0, 0, raw[:, ADA1 % RAW, :], free=False)
            conv_lo(0, 0)
            X, E, U, LN, SP_, LA, CUM, WX = range(8)
            dve.wait_ge(s_win, 1)
            dve.wait_ge(s_pack, 16 * 13)
            dve.tensor_scalar(dtw[:, X, :], banks[0][:, :], dtb[:, 0:1], None, ALU.add).then_inc(s_dtx, 1)
            dve.wait_ge(s_dtx, 1)
            dve.wait_ge(s_dexp, 2)
            dve.tensor_scalar(dtw[:, U, :], dtw[:, E, :], 1.0, None, ALU.add).then_inc(s_du, 1)
            dve.wait_ge(s_du, 1)
            ch(dve.tensor_scalar(dtw[:, SP_, :], dtw[:, U, :], 1.0, None, ALU.is_equal))
            ch(dve.scalar_tensor_tensor(dtw[:, LA, :], dtw[:, U, :], -1.0, dtw[:, SP_, :], ALU.add, ALU.add))
            ch(dve.reciprocal(dtw[:, LA, :], dtw[:, LA, :]))
            dve.wait_ge(s_dln, 1)
            ch(dve.tensor_tensor(dtw[:, LN, :], dtw[:, LN, :], dtw[:, SP_, :], ALU.add))
            ch(dve.tensor_tensor(dtw[:, LN, :], dtw[:, LN, :], dtw[:, LA, :], ALU.mult))
            ch(dve.tensor_tensor(dtw[:, LN, :], dtw[:, LN, :], dtw[:, E, :], ALU.mult))
            ch(dve.scalar_tensor_tensor(dtw[:, SP_, :], dtw[:, X, :], 0.0, dtw[:, LN, :], ALU.max, ALU.add))
            ch(dve.tensor_scalar(dtw[:, LA, :], dtw[:, SP_, :], arate[:, 0:1], -1.0, ALU.mult, ALU.mult))
            ch(dve.memset(dtw[:, U, :], 1.0))
            for a in (0, L):
                dve.tensor_tensor_scan(dtw[0:64, CUM, a:a + L], dtw[0:64, U, 0:L], dtw[0:64, LA, a:a + L], 0.0, ALU.mult, ALU.add)
                ch(dve.tensor_tensor_scan(dtw[64:128, CUM, a:a + L][:, ::-1], dtw[64:128, U, 0:L], dtw[64:128, LA, a:a + L][:, ::-1],
                                          0.0, ALU.mult, ALU.add))
            dve.tensor_copy(tot[0:64, :], dtw[0:64, CUM, T - 1:T])
            dve.tensor_copy(tot[64:128, :], dtw[64:128, CUM, L:L + 1]).then_inc(s_cumr, 1)
            dve.wait_ge(s_dw, 1)
            dve.tensor_tensor(dtw[:, WX, 0:LC], dtw[:, WX, 0:LC], dtw[:, SP_, L:T], ALU.mult).then_inc(s_dec, 1)
            dve.wait_ge(s_dtT, 1)
            tk = tokm[:, :, :, :].rearrange("p a d h -> p (a d h)")
            dve.tensor_copy(tk[:, 0:512], banks[3][:, :])
            dve.tensor_copy(tk[:, 512:768], banks[4][:, 0:256]).then_inc(s_tokm, 1)

            def store(g, n):
                kind, c = CHUNKS[n]
                dve.wait_ge(s_th, NCH * g + (n + 1))
                if kind == "C":
                    if not (isinstance(g, int) and g == 0):
                        dve.wait_ge(s_cb, g)
                    dst, w = cT[:, :], L
                elif kind == "z":
                    dst, w = zs[:, c, :], L
                else:
                    i = NTURN * g + (TURN_BEFORE[n] + 0)
                    if not (isinstance(g, int) and (g == 0 and TURN_BEFORE[n] <= 0)):
                        dve.wait_ge(s_T, i)
                    dst, w = slx[:, n % 2, :], T
                dve.scalar_tensor_tensor(dst, th[:, n % 2, 0:w], 1.0, cv[:, n % 2, 0:w], ALU.add, ALU.mult).then_inc(s_prod, 1)
                if kind == "B":
                    if not (isinstance(g, int) and g == 0):
                        dve.wait_ge(s_cb, g)
                    dve.wait_ge(s_prod, NCH * g + (n + 1))
                    dve.tensor_copy(bT[:, :], slx[:, n % 2, 0:L]).then_inc(s_bT, 1)

            def skip_term(g, n):
                c = CHUNKS[n][1]
                dve.wait_ge(s_prod, NCH * g + (n + 1))
                dve.tensor_scalar(dx[:, c, :], slx[:, n % 2, 0:L], dcol[:, bass.ds(GC * g + c, 1)], None, ALU.mult).then_inc(s_dx, 1)

            def differences(s, hf):
                i = 2 * s + (hf + 1)
                dve.wait_ge(s_bc, 32 * i)
                if hf == 1:
                    dve.wait_ge(s_y, GC * s + 2)
                for d in range(2):
                    for r in range(HALF):
                        q = d * HALF + r
                        j0, j1 = (tokg[:, 2 + j, d, HALF * hf + r:HALF * hf + r + 1] for j in range(2))
                        if d == 0:
                            a, b = (0, 2 * P, 0, L), (2 * P, WC, P, L)
                        else:
                            a, b = (0, P, 0, P), (P, WC, 0, L)
                        for (o0, o1, i0, i1), cj in ((a, j0), (b, j1)):
                            last = dve.tensor_scalar(wts[:, q, o0:o1], bc[:, q, i0:i1], cj, 0.0, ALU.subtract, ALU.min)
                last.then_inc(s_seg, 1)

            def weights(s, hf):
                i = 2 * s + (hf + 1)
                dve.wait_ge(s_expw, i)
                dve.wait_ge(s_cbm, s + 1)
                for d in range(2):
                    w = wts[:, d * HALF:(d + 1) * HALF, :]
                    last = dve.tensor_tensor(w, w, cbm[:, d:d + 1, :].broadcast_to([P, HALF, WC]), ALU.mult)
                last.then_inc(s_wts, 1)
                dve.wait_ge(s_ebc, i)
                dve.wait_ge(s_ct2, s + 1)
                dve.tensor_tensor(ce[:, :, :], ce[:, :, :], cT2[:, :].unsqueeze(1).broadcast_to([P, R, L]), ALU.mult).then_inc(s_ce, 1)

            def scaled_x(s):
                dve.wait_ge(s_Tev, NTURN * s + NTURN)
                dve.wait_ge(s_tg, s + 1)

                def by(k, d):
                    return tokg[:, k:k + 2, d, :].unsqueeze(3).broadcast_to([P, 2, R, 64])

                def heads(v):
                    return v.rearrange("p t (r e) -> p t r e", r=R)

                lat, con = heads(xtok[:, 0:2, :]), heads(xtok[:, 2:4, :])
                dve.tensor_tensor(heads(xdtf[:, :, :]), lat, by(0, 0), ALU.mult)
                dve.tensor_tensor(heads(xwf[:, :, :]), con, by(4, 0), ALU.mult)
                dve.tensor_tensor(lat, lat, by(0, 1), ALU.mult)
                dve.tensor_tensor(con, con, by(4, 1), ALU.mult).then_inc(s_xd, 1)

            def finish(s, c):
                dve.wait_ge(s_y, GC * s + (c + 1))
                dve.wait_ge(s_dx, GC * s + (c + 1))
                dve.wait_ge(s_yst[c % 2], 32 * s + (16 * (c // 2) + 16))
                dve.tensor_tensor(ybuf[:, c % 2, :], banks[6 + c % 2][:, 0:L], dx[:, c, :], ALU.add).then_inc(s_fin1, 1)
                dve.wait_ge(s_fin1, GC * s + (c + 1))
                dve.tensor_tensor(ybuf[:, c % 2, :], ybuf[:, c % 2, :], zs[:, c, :], ALU.mult).then_inc(s_fin2, 1)

            def masked(g):
                dve.wait_ge(s_cb, g + 1)
                c0, c1 = CBK[:, 0:L], CBK[:, L:2 * L]
                dve.tensor_tensor(cbm[:, 0, 0:P], c0[:, 0:P], tri_up[:, :], ALU.mult)
                dve.tensor_copy(cbm[:, 0, P:2 * P], c0[:, P:L])
                dve.tensor_tensor(cbm[:, 0, 2 * P:WC], c1[:, P:L], tri_up[:, :], ALU.mult)
                dve.tensor_tensor(cbm[:, 1, 0:P], c0[:, 0:P], tri_lo[:, :], ALU.mult)
                dve.tensor_copy(cbm[:, 1, P:2 * P], c1[:, 0:P])
                dve.tensor_tensor(cbm[:, 1, 2 * P:WC], c1[:, P:L], tri_lo[:, :], ALU.mult).then_inc(s_cbm, 1)

            def drain(g, n):
                kind = CHUNKS[n][0]
                slot, bank = n % 2, banks[(n + 1) % 2]
                if kind == "z":
                    dve.wait_ge(s_win, NCH * g + (n + 2))
                    dve.tensor_scalar(cv[:, slot, 0:L], bank[:, 0:L], 0.5, None, ALU.mult).then_inc(s_drain, 1)
                    return
                q = 2 if kind in "Bx" else 1
                o = cv[:, slot, 0:q * L].rearrange("p (q t) -> p q t", q=q)
                u = bank[:, 0:q * L].rearrange("p (q t) -> p q t", q=q)
                col = conv_col(g, n)
                i = NCONV * g + (CONV_AT[n] + 1)
                dve.wait_ge(s_cvA, i)
                dve.scalar_tensor_tensor(o[:, :, 1:L], u[:, :, 0:L - 1], tapc[:, 0, bass.ds(col, 1)], o[:, :, 1:L],
                                         ALU.mult, ALU.add).then_inc(s_cvB, 1)
                dve.wait_ge(s_cvB, i)
                dve.scalar_tensor_tensor(o[:, :, 0:L - 1], u[:, :, 1:L], tapc[:, 2, bass.ds(col, 1)], o[:, :, 0:L - 1],
                                         ALU.mult, ALU.add).then_inc(s_drain, 1)

            def steps(g, w, ssd):
                s = g - 1
                for n in range(NCH):
                    if w and n + 1 < NCH:
                        conv_lo(g, n + 1)
                    if w and n + 1 == NCH and not (isinstance(g, int) and g == GROUPS - 1):
                        conv_lo(g + 1, 0)
                    if ssd and n == 0:
                        dve.tensor_copy(tokg[:, :, :, :], tokm[:, :, :, bass.ds(R * s, R)]).then_inc(s_tg, 1)
                        dve.wait_ge(s_prod, NCH * s + 2)
                        dve.tensor_copy(cT2[:, :], cT[:, :]).then_inc(s_ct2, 1)
                        dve.wait_ge(s_tg, s + 1)
                        differences(s, 0)
                    if ssd and n == 4:
                        finish(s, 0)
                        finish(s, 1)
                        differences(s, 1)
                    if ssd and n == 7:
                        finish(s, 2)
                        finish(s, 3)
                    if ssd and n == 0:
                        store(s, NCH - 1)
                        skip_term(s, 8)
                    if w and n > 0:
                        store(g, n - 1)
                    if ssd and n == 1:
                        skip_term(s, 9)
                    if w and n == 4:
                        skip_term(g, 2)
                    if w and n == 7:
                        skip_term(g, 5)
                    if ssd and n in (1, 5):
                        weights(s, n // 5)
                    if w and n == 8:
                        masked(g)
                    if w and n == 9:
                        dve.wait_ge(s_ada, NADA * g + (ADA1 + NADA))
                        dve.tensor_tensor(ada2[:, bass.ds(NADA * g, NADA)], ADAK[:, 128:128 + NADA],
                                          packs[:, 0, bass.ds(NADA * g + ADA1, NADA)], ALU.add).then_inc(s_adaev, 1)
                    if w:
                        drain(g, n)
                    if ssd and n == 1:
                        scaled_x(s)

            dve.wait_ge(s_tokm, 1)
            dve.wait_ge(s_const, 6)
            steps(0, True, False)
            with dve.Fori(1, GROUPS - 1) as g:
                steps(g, True, True)
            steps(GROUPS - 1, True, True)
            steps(GROUPS, False, True)

            dve.wait_ge(s_adaev, GROUPS)
            dve.tensor_copy(a2c[:, :], ada2[:, :]).then_inc(s_a2, 1)
            dve.wait_ge(s_a2, 1)
            dve.scalar_tensor_tensor(a2c[:, 2 * KC:3 * KC], ada2[:, 2 * KC:3 * KC], 1.0, g1col, ALU.add, ALU.mult).then_inc(s_a2, 1)
            dve.wait_ge(s_a2T, 1)
            dve.tensor_copy(a2row[:, :], banks[3][0:ADA2, 0:P]).then_inc(s_a2r, 1)
            dve.wait_ge(s_yss, IC)
            for tt in range(TT):
                last = dve.tensor_scalar(ssq[:, tt:tt + 1], banks[(2, 4)[tt]][:, 0:1], 1.0 / DI, EPS, ALU.mult, ALU.add)
            last.then_inc(s_mean, 1)
            dve.wait_ge(s_rms, 2)
            dve.reciprocal(rstd[:, 4:6], rms[:, 4:6]).then_inc(s_rstd, 1)
            for k in range(IC):
                dve.wait_ge(s_yh, k + 1)
                dve.scalar_tensor_tensor(yl[:, k, :], yraw[:, k, :], ngcol[:, k:k + 1], yh[:, k, :].bitcast(F32),
                                         ALU.mult, ALU.subtract).then_inc(s_yl, 1)
                m = M_OUT + k
                dve.wait_ge(s_hi, m + 1)
                if k >= 2:
                    dve.wait_ge(s_wo, k - 1)
                dve.tensor_tensor(wlo[:, m % 2, :], raw[:, (OUT0 + k) % RAW, :], whi[:, m % 2, :].bitcast(F32),
                                  ALU.subtract).then_inc(s_lo, 1)
            dve.wait_ge(s_wo, IC)
            dve.wait_ge(s_rstd, 2)
            dve.wait_ge(s_modb, 48)
            dve.wait_ge(s_xres, 16)
            for q in range(8):
                tt, nb = q // 4, slice(q % 4 * 512, q % 4 * 512 + 512)
                dve.scalar_tensor_tensor(h2[:, tt, nb], banks[q][:, :], rstd[:, 4 + tt:5 + tt], gate_b[:, nb],
                                         ALU.mult, ALU.mult).then_inc(s_x1a, 1)
                dve.wait_ge(s_x1a, q + 1)
                dve.tensor_tensor(x1[:, tt, nb], x1[:, tt, nb], h2[:, tt, nb], ALU.add).then_inc(s_x1, 1)
            dve.wait_ge(s_ssq, 6)
            dve.tensor_scalar(ssq[:, 4:6], ssq[:, 2:4], 1.0 / D, EPS, ALU.mult, ALU.add).then_inc(s_mean, 1)
            dve.wait_ge(s_rms, 3)
            dve.reciprocal(rstd[:, 6:8], rms[:, 6:8]).then_inc(s_rstd, 1)
            dve.wait_ge(s_rstd, 3)
            for tt in range(TT):
                dve.scalar_tensor_tensor(h2[:, tt, :], x1[:, tt, :], rstd[:, 6 + tt:7 + tt], scale_b[:, :],
                                         ALU.mult, ALU.mult).then_inc(s_h2a, 1)
                dve.wait_ge(s_h2a, tt + 1)
                dve.tensor_tensor(h2[:, tt, :], h2[:, tt, :], shift_b[:, :], ALU.add).then_inc(s_h2, 1)
            for k in range(0, KC, 2):
                dve.wait_ge(s_h2t, k + 1)
                dve.tensor_copy(h2T[:, k, :], banks[k % 2][:, 0:L]).then_inc(s_h2tV, 1)

            dve.wait_ge(s_rwl, 64)
            dve.wait_ge(s_iota, 2)
            for tt in range(TT):
                lg = rt[:, tt, 0:2, :].rearrange("p a b -> p (a b)")
                dve.wait_ge(s_logit, tt + 1)
                ch(dve.tensor_tensor(lg[:, 0:NG + NE], banks[6 + tt][:, 0:NG + NE], rbias[:, :], ALU.add))
                ch(dve.memset(rt[:, tt, 7, 0:8], NEG))
                ch(dve.tensor_copy(rt[:, tt, 7, 0:NG], lg[:, 0:NG]))
                ch(dve.max(rt[:, tt, 2, 0:8], rt[:, tt, 7, 0:8]))
                dve.tensor_scalar(rt[:, tt, 2, 8:9], rt[:, tt, 2, 0:1], -1.0, None, ALU.mult).then_inc(s_gmax, 1)
                ch(dve.max_index(ridx[:, tt, 0, :], rt[:, tt, 2, 0:8], rt[:, tt, 7, 0:8]))
                ch(dve.tensor_copy(rt[:, tt, 6, 2:3], ridx[:, tt, 0, 0:1]))
                ch(dve.tensor_scalar(rt[:, tt, 6, 3:4], rt[:, tt, 6, 2:3], float(EPG), None, ALU.mult))
                ch(dve.tensor_scalar(rt[:, tt, 6, 4:5], rt[:, tt, 6, 3:4], float(EPG), None, ALU.add))
                ch(dve.tensor_scalar(rt[:, tt, 8, :], iota_e[:, :], rt[:, tt, 6, 3:4], None, ALU.is_ge))
                ch(dve.scalar_tensor_tensor(rt[:, tt, 8, :], iota_e[:, :], rt[:, tt, 6, 4:5], rt[:, tt, 8, :], ALU.is_lt, ALU.mult))
                ch(dve.tensor_tensor(rt[:, tt, 4, :], lg[:, NG:NG + NE], rt[:, tt, 8, :], ALU.mult))
                ch(dve.tensor_scalar(rt[:, tt, 9, :], rt[:, tt, 8, :], -NEG, NEG, ALU.mult, ALU.add))
                ch(dve.tensor_tensor(rt[:, tt, 4, :], rt[:, tt, 4, :], rt[:, tt, 9, :], ALU.add))
                ch(dve.max(rt[:, tt, 5, 0:8], rt[:, tt, 4, :]))
                dve.tensor_tensor(rt[:, tt, 3, 9:10], rt[:, tt, 5, 1:2], rt[:, tt, 5, 0:1], ALU.subtract).then_inc(s_ediff, 1)
                ch(dve.max_index(ridx[:, tt, 1, :], rt[:, tt, 5, 0:8], rt[:, tt, 4, :]))
                ch(dve.tensor_copy(rt[:, tt, 6, 0:2], ridx[:, tt, 1, 0:2]))
                for i in range(2):
                    ch(dve.tensor_scalar(pick[:, tt, i, :], iota_e[:, :], rt[:, tt, 6, i:i + 1], None, ALU.is_equal))
                dve.tensor_tensor(pick[:, tt, 2, :], pick[:, tt, 0, :], pick[:, tt, 1, :], ALU.add).then_inc(s_pick, 1)
            CNT, START, NB, BEND, BBEG, OH, OFF, COL, T0 = range(9)
            dve.wait_ge(s_rank, 1)
            ch(dve.memset(rs[:, T0, :], 1.0))
            ch(dve.tensor_copy(rs[:, CNT, :], banks[2][:, 0:NE]))
            ch(dve.tensor_tensor_scan(rs[:, START, :], rs[:, T0, :], rs[:, CNT, :], 0.0, ALU.mult, ALU.add))
            ch(dve.tensor_tensor(rs[:, START, :], rs[:, START, :], rs[:, CNT, :], ALU.subtract))
            ch(dve.tensor_scalar(rs[:, NB, :], rs[:, CNT, :], 0.0, None, ALU.is_gt))
            for q in range(1, L // SLOTS):
                ch(dve.scalar_tensor_tensor(rs[:, NB, :], rs[:, CNT, :], float(q * SLOTS), rs[:, NB, :], ALU.is_gt, ALU.add))
            ch(dve.tensor_tensor_scan(rs[:, BEND, :], rs[:, T0, :], rs[:, NB, :], 0.0, ALU.mult, ALU.add))
            ch(dve.tensor_tensor(rs[:, BBEG, :], rs[:, BEND, :], rs[:, NB, :], ALU.subtract))
            ch(dve.tensor_scalar(rs[:, OH, :], rs[:, BBEG, :], pidx[:, 0:1], None, ALU.is_le))
            ch(dve.scalar_tensor_tensor(rs[:, OH, :], rs[:, BEND, :], pidx[:, 0:1], rs[:, OH, :], ALU.is_gt, ALU.mult))
            ch(dve.scalar_tensor_tensor(rs[:, OFF, :], rs[:, BBEG, :], -float(SLOTS), rs[:, START, :], ALU.mult, ALU.add))
            ch(dve.tensor_tensor(rs[:, OFF, :], rs[:, OFF, :], rs[:, OH, :], ALU.mult))
            ch(dve.tensor_tensor(rs[:, OH, :], rs[:, OH, :], iota_e[:, :], ALU.mult))
            ch(dve.tensor_reduce(rs[:, COL, 0:1], rs[:, OH, :], AX_X, ALU.add))
            ch(dve.tensor_reduce(rs[:, COL, 3:4], rs[:, OFF, :], AX_X, ALU.add))
            ch(dve.scalar_tensor_tensor(rs[:, COL, 1:2], pidx[:, 0:1], float(SLOTS), rs[:, COL, 3:4], ALU.mult, ALU.add))
            ch(dve.tensor_scalar(rs[:, COL, 1:2], rs[:, COL, 1:2], float(ROWS), None, ALU.min))
            dve.tensor_copy(rs[:, COL, 2:3], rs[:, BEND, NE - 1:NE]).then_inc(s_tabc, 1)
            dve.wait_ge(s_tabr, 1)
            dve.tensor_copy(itab[0:1, :], banks[3][0:1, 0:3 * P]).then_inc(s_tab, 1)
            for tt in range(TT):
                ch(dve.tensor_tensor(rt[:, tt, 7, :], rs[:, START, :], banks[2][:, NE * (tt + 1):NE * (tt + 2)], ALU.add))
                for i in range(2):
                    ch(dve.tensor_tensor(rt[:, tt, 8, :], pick[:, tt, i, :], rt[:, tt, 7, :], ALU.mult))
                    ch(dve.tensor_reduce(rt[:, tt, 6, 8 + i:9 + i], rt[:, tt, 8, :], AX_X, ALU.add))
                ch(dve.tensor_scalar(onehot[:, tt, :], iota_r[:, 0:ROWS], rt[:, tt, 6, 8:9], None, ALU.is_equal))
                dve.scalar_tensor_tensor(onehot[:, tt, :], iota_r[:, 0:ROWS], rt[:, tt, 6, 9:10], onehot[:, tt, :],
                                         ALU.is_equal, ALU.add).then_inc(s_place, 1)
            for tt in range(TT):
                dve.wait_ge(s_gexp, tt + 1)
                dve.wait_ge(s_eexp, tt + 1)
                r = rt[:, tt, 3, 10:11]
                ch(dve.scalar_tensor_tensor(rt[:, tt, 10, 0:1], r, 1.0, rt[:, tt, 3, 8:9], ALU.add, ALU.mult))
                ch(dve.reciprocal(rt[:, tt, 10, 1:2], rt[:, tt, 10, 0:1]))
                ch(dve.tensor_tensor(rt[:, tt, 10, 2:3], rt[:, tt, 10, 1:2], r, ALU.mult))
                ch(dve.tensor_scalar(wonehot[:, tt, :], iota_r[:, 0:ROWS], rt[:, tt, 6, 8:9], rt[:, tt, 10, 1:2], ALU.is_equal, ALU.mult))
                ch(dve.tensor_scalar(oh_tmp[:, tt, :], iota_r[:, 0:ROWS], rt[:, tt, 6, 9:10], rt[:, tt, 10, 2:3], ALU.is_equal, ALU.mult))
                dve.tensor_tensor(wonehot[:, tt, :], wonehot[:, tt, :], oh_tmp[:, tt, :], ALU.add).then_inc(s_place, 1)
            for k in range(0, KC, 2):
                dve.wait_ge(s_xg, k + 1)
                dve.tensor_copy(xgT[:, k, 0:ROWS], banks[4 + k % 4][:, :]).then_inc(s_xgV, 1)
            for q in range(2):
                dve.wait_ge(s_gTp, q + 1)
                dve.tensor_copy(gT[:, 2 * q:2 * q + 2, :].rearrange("p a b -> p (a b)"), banks[q][:, :]).then_inc(s_gTv, 1)

            dve.wait_ge(s_xgA, KC // 2)
            dve.wait_ge(s_xgV, KC // 2)
            dve.wait_ge(s_pad, 1)
            dve.wait_ge(s_tab, 1)
            nblk = dve.value_load(itab[0:1, 2 * P:2 * P + 1], min_val=1, max_val=P)
            start0 = dve.value_load(itab[0:1, P:P + 1], min_val=0, max_val=ROWS)
            dve.tensor_copy(xe[:, :, :], xgT[:, :, bass.ds(start0, SLOTS)]).then_inc(s_xe, 1)
            with dve.Fori(0, nblk) as b:
                start = dve.value_load(itab[0:1, bass.ds(b + P, 1)], min_val=0, max_val=ROWS)
                after = dve.value_load(itab[0:1, bass.ds(b + (P + 1), 1)], min_val=0, max_val=ROWS)
                dve.wait_ge(s_gt, b + 1)
                dve.scalar_tensor_tensor(gsil[:, :, :].rearrange("p f n -> p (f n)"), gtanh[:, :, :].rearrange("p f n -> p (f n)"), 1.0,
                                         banks[0][:, 0:FC * SLOTS], ALU.add, ALU.mult).then_inc(s_gs, 1)
                dve.wait_ge(s_use[UP], b + 2)
                dve.wait_ge(s_gs, b + 1)
                dve.scalar_tensor_tensor(hdn[:, :, :].rearrange("p f n -> p (f n)"), gsil[:, :, :].rearrange("p f n -> p (f n)"), 0.5,
                                         banks[1][:, 0:FC * SLOTS], ALU.mult, ALU.mult).then_inc(s_hd, 1)
                dve.tensor_copy(xe[:, :, :], xgT[:, :, bass.ds(after, SLOTS)]).then_inc(s_xe, 1)
                dve.wait_ge(s_use[DOWN], b + 2)
                dve.tensor_copy(outT[:, KC // 2:KC, bass.ds(start, SLOTS)],
                                banks[3][:, :].rearrange("p (c n) -> p c n", c=KC // 2)).then_inc(s_oV, 1)
            dve.wait_ge(s_g5, 16)
            for q in range(8):
                tt, nb = q // 4, slice(q % 4 * 512, q % 4 * 512 + 512)
                dve.wait_ge(s_fy, q + 1)
                dve.tensor_tensor(ctmp[:, q % 2, :], banks[4 + q % 4][:, :], gate5_b[:, nb], ALU.mult).then_inc(s_f1, 1)
                dve.wait_ge(s_f1, q + 1)
                if q >= 2:
                    dve.wait_ge(s_out[q % 2], 16 * (q // 2))
                dve.tensor_tensor(fin[:, q % 2, :], ctmp[:, q % 2, :], x1[:, tt, nb], ALU.add).then_inc(s_f2, 1)

        @block.tensor
        def _(pe):
            pe.wait_ge(s_const, 6)
            pe.wait_ge(s_pack, 16 * 13)
            for i in range(3):
                last = pe.transpose(banks[3][:, P * i:P * i + P], prow[:, i, :], ident[:, :])
            last.then_inc(s_ptr, 1)
            for k in range(KC):
                if k >= 2:
                    pe.wait_ge(s_xte, k - 1)
                for tt in range(4):
                    if k == 0:
                        pe.wait_ge(s_xn, tt + 1)
                    last = pe.transpose(banks[k % 2][:, P * tt:P * tt + P], xrows[:, tt, P * k:P * k + P], ident[:, :])
                last.then_inc(s_xt, 1)
            pe.wait_ge(s_cvec, 1)
            for a in range(ADA1):
                pe.wait_ge(s_raw[a % RAW], 16 * (a // RAW + 1))
                tile = w_view(raw, a % RAW)
                for k in range(KC):
                    last = pe.matmul(ADAK[:, 2 * a:2 * a + 2], tile[:, k, :], cvec[:, k, :], start=(k == 0), stop=(k == KC - 1))
                last.then_inc(s_ada, 1)

            def project(bank, slot, width, inc, k_wait=None):
                wh, wl = w_view(whi, slot), w_view(wlo, slot)
                for k in range(KC):
                    if k_wait:
                        pe.wait_ge(s_hl, k + 1)
                    pe.matmul(bank[:, 0:width], wh[:, k, :], hTh[:, k, 0:width], start=(k == 0), stop=False)
                    pe.matmul(bank[:, 0:width], wh[:, k, :], hTl[:, k, 0:width], start=False, stop=False)
                    last = pe.matmul(bank[:, 0:width], wl[:, k, :], hTh[:, k, 0:width], start=False, stop=(k == KC - 1))
                last.then_inc(inc, 1)

            pe.wait_ge(s_lo, 1)
            project(banks[0], 0, T, s_win, k_wait=True)
            pe.wait_ge(s_dec, 1)
            for i, (q, a) in enumerate(((4, 0), (4, P), (6, 0), (6, P))):
                pe.transpose(banks[3][:, P * i:P * i + P], dtw[:, q, a:a + P], ident[:, :])
            for i in range(2):
                last = pe.transpose(banks[4][:, P * i:P * i + P], dtw[:, 7, P * i:P * i + P], ident[:, :])
            last.then_inc(s_dtT, 1)
            pe.wait_ge(s_tokm, 1)

            def turn(g, n):
                i = NTURN * g + TURN_AT[n]
                pe.wait_ge(s_prod, NCH * g + (n + 1))
                if not (isinstance(g, int) and g == 0 and n == 0):
                    pe.wait_ge(s_Tev, i)
                if n == 0:
                    tiles = [(0, L), (1, L + P)]
                else:
                    tiles = [(q, P * q) for q in range(4)]
                for q, a in tiles:
                    last = pe.transpose(TURN[:, P * q:P * q + P], slx[:, n % 2, a:a + P], ident[:, :])
                last.then_inc(s_T, 1)

            def states(s):
                pe.wait_ge(s_xd, s + 1)
                pe.wait_ge(s_cbm, s + 1)
                for d in range(2):
                    for j in range(2):
                        rhs = xwf[:, j, :] if d == 0 else xtok[:, 2 + j, :]
                        last = pe.matmul(STK[d][:, :], btok[:, j, :], rhs, start=(j == 0), stop=(j == 1))
                last.then_inc(s_st, 1)

            def y_chunk(s, c):
                hf = c // 2
                pe.wait_ge(s_wts, 2 * s + (hf + 1))
                pe.wait_ge(s_ce, 2 * s + (hf + 1))
                pe.wait_ge(s_stev, s + 1)
                if c >= 2:
                    pe.wait_ge(s_fin1, GC * s + (c - 1))
                for r in (2 * c, 2 * c + 1):
                    o = banks[6 + c % 2][64 * (r % 2):64 * (r % 2) + 64, 0:L]
                    hs = slice(64 * r, 64 * r + 64)
                    for d in range(2):
                        q = d * HALF + r % HALF
                        pe.matmul(o, st[:, d, hs], ce[:, q, :], start=(d == 0), stop=False)
                        if d == 0:
                            pe.matmul(o, xdtf[:, 0, hs], wts[:, q, 0:2 * P], start=False, stop=False)
                            pe.matmul(o[:, P:L], xdtf[:, 1, hs], wts[:, q, 2 * P:WC], start=False, stop=False)
                        else:
                            pe.matmul(o[:, 0:P], xtok[:, 0, hs], wts[:, q, 0:P], start=False, stop=False)
                            last = pe.matmul(o, xtok[:, 1, hs], wts[:, q, P:WC], start=False, stop=True)
                last.then_inc(s_y, 1)

            def c_times_b(g):
                pe.wait_ge(s_bT, g + 1)
                pe.wait_ge(s_prod, NCH * g + 2)
                if not (isinstance(g, int) and g == 0):
                    pe.wait_ge(s_stev, g)
                for j in range(2):
                    last = pe.matmul(CBK[:, L * j:L * j + L], bT[:, P * j:P * j + P], cT[:, :], start=True, stop=True)
                last.then_inc(s_cb, 1)

            def steps(g, w, ssd):
                s = g - 1
                for n in range(NCH):
                    if w:
                        m = NCH * g + (n + 1)
                        pe.wait_ge(s_hi, m + 1)
                        pe.wait_ge(s_lo, m + 1)
                        if isinstance(g, int) and g == 0 and n == 0:
                            pass
                        elif isinstance(g, int) and g == 0 and n == 1:
                            pe.wait_ge(s_dtx, 1)
                        else:
                            pe.wait_ge(s_drain, NCH * g + (n - 1))
                        project(banks[(n + 1) % 2], (n + 1) % 2, T if CHUNKS[n][0] in "Bx" else L, s_win)
                    if ssd and n in (0, 1):
                        turn(s, (8, 9)[n])
                    if ssd and n == 2:
                        states(s)
                    if w and n in (2, 4, 7):
                        turn(g, {2: 0, 4: 2, 7: 5}[n])
                    if ssd and n in (3, 6):
                        y_chunk(s, 0 if n == 3 else 2)
                        y_chunk(s, 1 if n == 3 else 3)
                    if w and n == 7:
                        c_times_b(g)
                    if w and n < NADA:
                        pos = POS[("a", n)]
                        pe.wait_ge(s_raw[raw_of(pos)], raw_count(group_raw(g), pos))
                        if n == 0 and not (isinstance(g, int) and g == 0):
                            pe.wait_ge(s_adaev, g)
                        tile = w_view(raw, raw_of(pos))
                        for k in range(KC):
                            last = pe.matmul(ADAK[:, 128 + n:129 + n], tile[:, k, :], cvec[:, k, 0:1], start=(k == 0), stop=(k == KC - 1))
                        last.then_inc(s_ada, 1)

            steps(0, True, False)
            with pe.Fori(1, GROUPS - 1) as g:
                steps(g, True, True)
            steps(GROUPS - 1, True, True)
            steps(GROUPS, False, True)

            pe.wait_ge(s_a2, 2)
            pe.wait_ge(s_Tev, NTURN * GROUPS)
            pe.transpose(banks[3][0:ADA2, 0:P], a2c[:, :], ident[:, :]).then_inc(s_a2T, 1)
            pe.wait_ge(s_adaev, GROUPS)
            pe.wait_ge(s_stev, GROUPS)
            for k in range(IC):
                pe.wait_ge(s_ysq, k + 1)
                for tt in range(TT):
                    last = pe.matmul(banks[(2, 4)[tt]][:, 0:1], ysq[:, k % 2, P * tt:P * tt + P], ones[:, 0:1],
                                     start=(k == 0), stop=(k == IC - 1))
                last.then_inc(s_yss, 1)
            pe.wait_ge(s_mean, 2)
            pe.wait_ge(s_a2r, 1)
            pe.wait_ge(s_fin1, IC)
            for k in range(IC):
                m = M_OUT + k
                pe.wait_ge(s_yl, k + 1)
                pe.wait_ge(s_lo, m + 1)
                for tt in range(TT):
                    ys_, yls = yh[:, k, P * tt:P * tt + P], yl[:, k, P * tt:P * tt + P]
                    for a, ring, first, final in ((ys_, whi, True, False), (ys_, wlo, False, False), (yls, whi, False, True)):
                        for nb in range(4):
                            last = pe.matmul(banks[4 * tt + nb][:, :], a, ring[:, m % 2, 512 * nb:512 * nb + 512],
                                             start=(k == 0 and first), stop=(k == IC - 1 and final))
                last.then_inc(s_wo, 1)
            pe.wait_ge(s_h2, TT)
            for k in range(KC):
                if k >= 2:
                    pe.wait_ge(s_h2tV if k % 2 == 0 else s_h2tA, k // 2)
                for tt in range(TT):
                    last = pe.transpose(banks[k % 2][:, P * tt:P * tt + P], h2[:, tt, P * k:P * k + P], ident[:, :])
                last.then_inc(s_h2t, 1)
            pe.wait_ge(s_rwl, 64)
            pe.wait_ge(s_h2tV, KC // 2)
            pe.wait_ge(s_h2tA, KC // 2)
            for tt in range(TT):
                for k in range(KC):
                    last = pe.matmul(banks[6 + tt][:, 0:NG + NE], h2T[:, k, P * tt:P * tt + P], rw[:, k, :], start=(k == 0), stop=(k == KC - 1))
                last.then_inc(s_logit, 1)
            pe.wait_ge(s_pick, TT)
            pe.wait_ge(s_strict, 1)
            for tt in range(TT):
                pe.matmul(banks[2][:, 0:NE], ones[:, :], pick[:, tt, 2, :], start=(tt == 0), stop=(tt == 1))
            pe.matmul(banks[2][:, NE:2 * NE], strict[:, :], pick[:, 0, 2, :], start=True, stop=True)
            pe.matmul(banks[2][:, 2 * NE:3 * NE], ones[:, :], pick[:, 0, 2, :], start=True, stop=False)
            pe.matmul(banks[2][:, 2 * NE:3 * NE], strict[:, :], pick[:, 1, 2, :], start=False, stop=True).then_inc(s_rank, 1)
            pe.wait_ge(s_tabc, 1)
            for i in range(3):
                last = pe.matmul(banks[3][0:1, P * i:P * i + P], rs[:, 7, i:i + 1], ident[:, :], start=True, stop=True)
            last.then_inc(s_tabr, 1)
            pe.wait_ge(s_place, TT)
            for k in range(KC):
                if k >= 4:
                    pe.wait_ge(s_xgV if k % 2 == 0 else s_xgA, (k - 4) // 2 + 1)
                for tt in range(TT):
                    last = pe.matmul(banks[4 + k % 4][:, :], h2[:, tt, k:D:KC], onehot[:, tt, :], start=(tt == 0), stop=(tt == TT - 1))
                last.then_inc(s_xg, 1)
            pe.wait_ge(s_place, 2 * TT)
            for q in range(2):
                for i in range(2):
                    for tt in range(TT):
                        last = pe.transpose(banks[q][:, 256 * i + P * tt:256 * i + P * tt + P],
                                            wonehot[:, tt, P * (2 * q + i):P * (2 * q + i) + P], ident[:, :])
                last.then_inc(s_gTp, 1)
            pe.wait_ge(s_gTv, 2)
            pe.wait_ge(s_tab, 1)
            for i in range(6):
                pe.sem_inc(s_use[i], 1)
            nblk = pe.value_load(itab[0:1, 2 * P:2 * P + 1], min_val=1, max_val=P)
            with pe.Fori(0, nblk) as b:
                for u, (w, bank) in enumerate(((wg, banks[0]), (wu, banks[1]))):
                    if u == 0:
                        pe.wait_ge(s_xe, b + 1)
                    for hf in range(2):
                        pe.wait_ge(s_ld[2 * u + hf], b * 16 + 16)
                        for f in range(FC):
                            for k in range(hf * KC // 2, (hf + 1) * KC // 2):
                                last = pe.matmul(bank[:, SLOTS * f:SLOTS * f + SLOTS], w[:, k, P * f:P * f + P], xe[:, k, :],
                                                 start=(hf == 0 and f == 0 and k == 0), stop=(k == KC - 1), skip_group_check=True)
                        last.then_inc(s_use[2 * u + hf], 1)
                pe.wait_ge(s_hd, b + 1)
                for hf in range(2):
                    pe.wait_ge(s_ld[4 + hf], b * 16 + 16)
                    for f in range(hf * FC // 2, (hf + 1) * FC // 2):
                        for c in range(KC):
                            last = pe.matmul(banks[2 + c // 8][:, SLOTS * (c % 8):SLOTS * (c % 8) + SLOTS], wd[:, f, P * c:P * c + P],
                                             hdn[:, f, :], start=(f == 0 and c % 8 == 0), stop=(f == FC - 1), skip_group_check=True)
                    last.then_inc(s_use[4 + hf], 1)
            pe.wait_ge(s_oA, nblk)
            pe.wait_ge(s_oV, nblk)
            for q in range(4 * ROWS // P):
                if q >= 2:
                    pe.wait_ge(s_fTe, q - 1)
                for i in range(4):
                    last = pe.transpose(banks[q % 2][:, P * i:P * i + P], outT[:, q % 4 * 4 + i, q // 4 * P:q // 4 * P + P], ident[:, :])
                last.then_inc(s_fT, 1)
            pe.wait_ge(s_fTe, 4 * ROWS // P)
            for q in range(8):
                tt, nb = q // 4, q % 4
                if q >= 4:
                    pe.wait_ge(s_f1, q - 3)
                for i in range(ROWS // P):
                    last = pe.matmul(banks[4 + q % 4][:, :], gT[:, i, P * tt:P * tt + P], ys[:, i, 512 * nb:512 * nb + 512],
                                     start=(i == 0), stop=(i == ROWS // P - 1))
                last.then_inc(s_fy, 1)


_USED = ["x", "c", "ctx", "c_ctx", "ada_w", "ada_b", "norm_g", "ssm_w_in", "ssm_conv_w", "ssm_conv_b", "ssm_a_log",
         "ssm_dt_bias", "ssm_d", "ssm_norm_g", "ssm_w_out", "moe_w_group", "moe_b_group", "moe_w_expert", "moe_b_expert",
         "moe_w_gate", "moe_w_up", "moe_w_down"]


def kernel(**inputs):
    import numpy as _np
    import concourse.bacc as _bacc
    from concourse import mybir as _mybir
    from concourse.bass_utils import run_bass_kernel_spmd as _run

    nc = _bacc.Bacc("TRN2", target_bir_lowering=False, num_devices=1)
    arrays, t = {}, {}
    for name in _USED:
        a = _np.ascontiguousarray(inputs[name])
        arrays[f"in_{name}"] = a
        t[name] = nc.dram_tensor(f"in_{name}", a.shape, _mybir.dt.from_np(a.dtype), kind="ExternalInput").ap()
    shape = _np.shape(inputs["x"])
    t["out"] = nc.dram_tensor("out_0", shape, _mybir.dt.float32, kind="ExternalOutput").ap()
    build(nc, t)
    r = _run(nc, [arrays], core_ids=[0])
    return r.results[0]["out_0"]
```

```python
from contextlib import ExitStack

import numpy as np
import concourse.bass as bass
from concourse import mybir

F32 = mybir.dt.float32
F32R = mybir.dt.float32r
I32 = mybir.dt.int32
U32 = mybir.dt.uint32
ALU = mybir.AluOpType
ACT = mybir.ActivationFunctionType
AX_X = mybir.AxisListType.X

P = 128
EPS = 1e-6
NEG = -1.0e30

CHUNKS = [("B", 0), ("C", 0), ("x", 0), ("z", 0), ("z", 1), ("x", 1), ("z", 2), ("z", 3), ("x", 2), ("x", 3)]
NCH = len(CHUNKS)
CONV_AT = {0: 0, 1: 1, 2: 2, 5: 3, 8: 4, 9: 5}
TURN_AT = {0: 0, 2: 1, 5: 2, 8: 3, 9: 4}
NCONV, NTURN = len(CONV_AT), len(TURN_AT)
TURN_BEFORE = {0: -1, 2: 1, 5: 0, 8: 2, 9: 3}
NADA = 8
ADA_STEP = {0: 0, 1: 1, 2: 2, 3: 3, 5: 4, 6: 5, 7: 6, 8: 7}
LOADS = [("w", 0)] + [t for n in range(NCH - 1) for t in [("w", n + 1)] + ([("a", ADA_STEP[n])] if n in ADA_STEP else [])]
RAW = 3
SLOTS = 64


def build(nc, t):
    D = t["x"].shape[2]
    L = t["x"].shape[1]
    LC = t["ctx"].shape[1]
    T = L + LC
    KC = D // P
    TT = L // P
    DI = t["ssm_norm_g"].shape[1]
    IC = DI // P
    HEADS = t["ssm_d"].shape[1]
    CD = t["ssm_conv_w"].shape[2]
    GN = (CD - DI) // 2
    GROUPS = GN // P
    R = HEADS // GROUPS
    GC = IC // GROUPS
    NG, NE, EPG = t["moe_w_group"].shape[2], t["moe_w_expert"].shape[2], t["moe_w_expert"].shape[2] // t["moe_w_group"].shape[2]
    FF = t["moe_w_gate"].shape[3]
    FC = FF // P
    ROWS = 2 * L
    RPAD = ROWS + SLOTS
    ADA1 = 2 * KC
    ADA2 = 4 * KC
    NB1 = ADA1 // 4
    assert L == 256 and LC == 256 and R == 8 and GC == 4 and ADA2 == NADA * GROUPS and TT == 2
    PRE = ADA1 + 1
    assert PRE % RAW == 0 and len(LOADS) % RAW == 0
    OUT0 = PRE + len(LOADS) * GROUPS
    M_OUT = 1 + NCH * GROUPS
    HALF = R // 2
    QW = KC // 4
    NQ = 8
    HW, NH = QW // 2, 2 * NQ
    DOWN_ORDER = (1, 0, 2, 3)
    EL0 = NH
    RING = 6
    WC = 3 * P

    w_in = t["ssm_w_in"][0].rearrange("(k p) n -> p k n", p=P)
    ada_w = t["ada_w"][0].rearrange("(k p) n -> p k n", p=P)

    def ada_tile(blk, q):
        return ada_w[:, 4 * q:4 * q + 4, bass.ds(512 * blk, 512)]

    w_out = t["ssm_w_out"][0].rearrange("(k p) n -> k p n", p=P)
    w_gate = t["moe_w_gate"][0].rearrange("e (p c) n -> e p c n", c=KC)
    w_up = t["moe_w_up"][0].rearrange("e (p c) n -> e p c n", c=KC)
    w_down = t["moe_w_down"][0].rearrange("e (f p) n -> e p f n", p=P)
    Z0, X0, B0, C0, DT0 = 0, DI, 2 * DI, 2 * DI + GN, 2 * DI + 2 * GN

    def w_in_at(g, n):
        kind, c = CHUNKS[n]
        return {"z": Z0 + 512 * g + P * c, "x": X0 + 512 * g + P * c, "B": B0 + P * g, "C": C0 + P * g}[kind]

    def conv_col(g, n):
        kind, c = CHUNKS[n]
        return {"x": GC * g + c, "B": IC + g, "C": IC + GROUPS + g}[kind]

    with ExitStack() as ctx:
        def sb(name, shape, dt=F32):
            return ctx.enter_context(nc.sbuf_tensor(name, shape, dt))

        def sem(name):
            return ctx.enter_context(nc.semaphore(name))

        ident = sb("ident", [P, P])
        ones = sb("ones", [P, P])
        tri_up = sb("tri_up", [P, P])
        tri_lo = sb("tri_lo", [P, P])
        pidx = sb("pidx", [P, 1])
        packs = sb("packs", [P, 3, P])
        adab = packs[:, 0, 0:96]
        g0col, g1col = packs[:, 1, 96:112], packs[:, 1, 112:128]
        ngcol = packs[:, 2, 96:128]
        tapc = sb("tapc", [P, 4, 48])
        cvec = sb("cvec", [P, KC, 2])
        cth = sb("cth", [P, KC, 2])
        adac = sb("adac", [P, 2 * KC, 2])
        acol = sb("acol", [P, KC, 2])
        arow = sb("arow", [P, 512])
        dcol = sb("dcol", [P, IC])
        dtb = sb("dtb", [P, 1])
        alog = sb("alog", [P, 1])
        arate = sb("arate", [P, 1])
        tot = sb("tot", [P, 1])
        ssq = sb("ssq", [P, 8])
        rms = sb("rms", [P, 8])
        rstd = sb("rstd", [P, 8])
        tokm = sb("tokm", [P, 6, 2, HEADS])
        tokg = sb("tokg", [P, 6, 2, R])

        KB = 1024
        base = (nc.sbuf_base + 63) // 64 * 64
        ARENA = 197 * KB
        arena = ctx.enter_context(nc.sbuf_tensor("arena", [P, (ARENA + 64) // 4], F32))

        def at(name, kb, shape, dt=F32):
            size = int(np.prod(shape[1:])) * 4
            assert kb * KB + size <= ARENA, name
            return nc.alloc_sbuf_tensor_at(name, shape, dt, offset=base + int(kb * KB))

        hTh = at("hTh", 0, [P, KC, T], F32R)
        hTl = at("hTl", 32, [P, KC, T], F32R)
        raw = at("raw", 64, [P, RAW, D])
        whi = at("whi", 88, [P, 2, D], F32R)
        wlo = at("wlo", 104, [P, 2, D], F32R)
        xtok = at("xtok", 120, [P, 4, 512])
        xdtf = at("xdtf", 128, [P, TT, 512])
        xwf = at("xwf", 132, [P, TT, 512])
        bc = at("bc", 136, [P, R, L])
        ce = at("ce", 144, [P, R, L])
        wts = at("wts", 152, [P, R, WC])
        zs = at("zs", 164, [P, GC, L])
        dx = at("dx", 168, [P, GC, L])
        st = at("st", 172, [P, 2, 512])
        bT = at("bT", 176, [P, L])
        cT = at("cT", 177, [P, L])
        cT2 = at("cT2", 178, [P, L])
        btok = at("btok", 179, [P, TT, P])
        cv = at("cv", 180, [P, 2, T])
        th = at("th", 184, [P, 2, T])
        slx = at("slx", 188, [P, 2, T])
        cbm = at("cbm", 192, [P, 2, WC])
        ybuf = at("ybuf", 195, [P, 2, L])
        xrows = at("xrows", 120, [P, 4, D])
        xnT = at("xnT", 152, [P, KC, T])
        prow = at("prow", 184, [P, 3, P])
        sqr0 = at("sqr0", 186, [P, D])
        dtw = at("dtw", 120, [P, 8, T])
        a1rows = at("a1rows", 0, [2, NB1, 512])
        a1in = at("a1in", 16, [2 * ADA1, P])
        yraw = at("yraw", 0, [P, IC, L])
        yh = at("yh", 32, [P, IC, L], F32R)
        yl = at("yl", 120, [P, IC, L], F32R)
        ysq = at("ysq", 152, [P, 2, L])
        a2row = at("a2row", 154, [ADA2, P])
        ada2 = at("ada2", 157, [P, ADA2])
        a2c = at("a2c", 156, [P, ADA2])
        gate_b = at("gate_b", 164, [P, D])
        scale_b = at("scale_b", 172, [P, D])
        shift_b = at("shift_b", 180, [P, D])
        x1 = at("x1", 0, [P, TT, D])
        h2 = at("h2", 16, [P, TT, D])
        sqr1 = at("sqr1", 120, [P, D])
        h2T = at("h2T", 32, [P, KC, L])
        rw = at("rw", 188, [P, KC, NG + NE])
        rbias = at("rbias", 190.5, [P, NG + NE])
        iota_r = at("iota_r", 194, [P, RPAD])
        strict = at("strict", 193, [P, P])
        iota_e = at("iota_e", 51, [P, NE])
        rt = at("rt", 48, [P, TT, 11, NE])
        pick = at("pick", 186, [P, TT, 3, NE])
        rs = at("rs", 184, [P, 12, NE])
        ridx = at("ridx", 187, [P, TT, 2, 8], U32)
        onehot = at("onehot", 32, [P, TT, ROWS], F32R)
        h2h = at("h2h", 120, [P, TT, D], F32R)
        h2l = at("h2l", 136, [P, TT, D], F32R)
        wonehot = at("wonehot", 36, [P, TT, ROWS])
        oh_tmp = at("oh_tmp", 40, [P, TT, ROWS])
        wd = at("wd", 16, [P, FC, D])
        gsb = at("gsb", 48, [P, FF])
        usb = at("usb", 50, [P, FF])
        xgT = at("xgT", 52, [P, KC, RPAD])
        wr = [at(f"wr{i}", kb, [P, QW, FF]) for i, kb in enumerate((88, 96, 104, 112, 152, 160))]
        eh = at("eh", 120, [P, 4, HW, FF], F32R)
        el = at("el", 136, [P, 4, HW, FF], F32R)
        xs = at("xs", 168, [P, KC, 2 * SLOTS], F32R)
        osb = at("osb", 176, [SLOTS, D])
        gT = at("gT", 184, [P, ROWS // P, L])
        itab = at("itab", 188, [1, 3 * P], I32)
        stack2 = at("stack2", 189.5, [P, SLOTS])
        hdn = at("hdn", 190, [P, FC, SLOTS])
        gtanh = at("gtanh", 191, [P, FC, SLOTS])
        gsil = at("gsil", 192, [P, FC, SLOTS])
        xe = at("xe", 193, [P, KC, SLOTS])
        ys = at("ys", 88, [P, ROWS // P, D])
        gate5_b = at("gate5_b", 120, [P, D])
        ctmp = at("ctmp", 128, [P, 2, 512])
        fin = at("fin", 132, [P, 2, 512])

        banks = [ctx.enter_context(nc.psum_tensor(f"bank{i}", [P, 512], F32)) for i in range(8)]
        TURN, CBK, STK = banks[3], banks[4], [banks[5], banks[4]]
        ADAK = banks[2]

        cum_d = nc.dram_tensor("cum_d", (P, L), F32, kind="Internal").ap()
        y_d = nc.dram_tensor("y_d", (DI, L), F32, kind="Internal").ap()
        mod1_d = nc.dram_tensor("mod1_d", (2, NB1 * 512), F32, kind="Internal").ap()
        mod2_d = nc.dram_tensor("mod2_d", (ADA2 // 4, 512), F32, kind="Internal").ap()
        rows_d = nc.dram_tensor("rows_d", (RPAD, D), F32, kind="Internal").ap()
        mod_d = nc.dram_tensor("mod_d", (ADA2, P), F32, kind="Internal").ap()

        s_pack = sem("s_pack")
        s_x = sem("s_x")
        s_const = sem("s_const")
        s_raw = [sem(f"s_raw{i}") for i in range(RAW)]
        s_ptr = sem("s_ptr")
        s_pk = sem("s_pk")
        s_cth = sem("s_cth")
        s_cvec = sem("s_cvec")
        s_ssq = sem("s_ssq")
        s_mean = sem("s_mean")
        s_rms = sem("s_rms")
        s_rstd = sem("s_rstd")
        s_xn = sem("s_xn")
        s_xt = sem("s_xt")
        s_xte = sem("s_xte")
        s_ada = sem("s_ada")
        s_bT = sem("s_bT")
        s_h = sem("s_h")
        s_hh = sem("s_hh")
        s_hl = sem("s_hl")
        s_hi = sem("s_hi")
        s_lo = sem("s_lo")
        s_win = sem("s_win")
        s_drain = sem("s_drain")
        s_cvA = sem("s_cvA")
        s_cvB = sem("s_cvB")
        s_th = sem("s_th")
        s_prod = sem("s_prod")
        s_T = sem("s_T")
        s_Tev = sem("s_Tev")
        s_dx = sem("s_dx")
        s_dtx = sem("s_dtx")
        s_dabs = sem("s_dabs")
        s_dexp = sem("s_dexp")
        s_du = sem("s_du")
        s_dln = sem("s_dln")
        s_cumr = sem("s_cumr")
        s_dw = sem("s_dw")
        s_dec = sem("s_dec")
        s_dtT = sem("s_dtT")
        s_tokm = sem("s_tokm")
        s_bc = sem("s_bc")
        s_cb = sem("s_cb")
        s_cbm = sem("s_cbm")
        s_tg = sem("s_tg")
        s_ct2 = sem("s_ct2")
        s_seg = sem("s_seg")
        s_expw = sem("s_expw")
        s_ebc = sem("s_ebc")
        s_wts = sem("s_wts")
        s_ce = sem("s_ce")
        s_xd = sem("s_xd")
        s_st = sem("s_st")
        s_stev = sem("s_stev")
        s_y = sem("s_y")
        s_fin1 = sem("s_fin1")
        s_fin2 = sem("s_fin2")
        s_yst = [sem(f"s_yst{i}") for i in range(2)]
        s_a1e = sem("s_a1e")
        s_a1s = sem("s_a1s")
        s_a1l = sem("s_a1l")
        s_a1T = sem("s_a1T")
        s_acc = sem("s_acc")
        s_ada2 = sem("s_ada2")
        s_asum = sem("s_asum")
        s_adaev = sem("s_adaev")
        s_ads = sem("s_ads")
        s_a2in = sem("s_a2in")
        s_a2p = sem("s_a2p")
        s_yld = [sem(f"s_yld{i}") for i in range(GROUPS)]
        s_ysq = sem("s_ysq")
        s_yss = sem("s_yss")
        s_yt = sem("s_yt")
        s_yh = sem("s_yh")
        s_yl = sem("s_yl")
        s_a2 = sem("s_a2")
        s_a2T = sem("s_a2T")
        s_a2r = sem("s_a2r")
        s_mod = sem("s_mod")
        s_modb = sem("s_modb")
        s_xres = sem("s_xres")
        s_wo = sem("s_wo")
        s_x1a = sem("s_x1a")
        s_x1 = sem("s_x1")
        s_h2a = sem("s_h2a")
        s_h2 = sem("s_h2")
        s_h2h = sem("s_h2h")
        s_h2t = sem("s_h2t")
        s_h2tA = sem("s_h2tA")
        s_h2tV = sem("s_h2tV")
        s_logit = sem("s_logit")
        s_gmax = sem("s_gmax")
        s_gexp = sem("s_gexp")
        s_ediff = sem("s_ediff")
        s_eexp = sem("s_eexp")
        s_pick = sem("s_pick")
        s_rank = sem("s_rank")
        s_tabc = sem("s_tabc")
        s_tabr = sem("s_tabr")
        s_place = sem("s_place")
        s_gTp = sem("s_gTp")
        s_gTv = sem("s_gTv")
        s_rwl = sem("s_rwl")
        s_iota = sem("s_iota")
        s_xg = sem("s_xg")
        s_xgA = sem("s_xgA")
        s_xgV = sem("s_xgV")
        s_tab = sem("s_tab")
        s_v = sem("s_v")
        s_wr = [sem(f"s_wr{i}") for i in range(RING)]
        s_wd = [sem(f"s_wd{i}") for i in range(FC)]
        s_eh = sem("s_eh")
        s_el = sem("s_el")
        s_gu = sem("s_gu")
        s_xe = sem("s_xe")
        s_xh = sem("s_xh")
        s_xs = sem("s_xs")
        s_gc = sem("s_gc")
        s_uc = sem("s_uc")
        s_gt = sem("s_gt")
        s_ut = sem("s_ut")
        s_th2 = sem("s_th2")
        s_gs = sem("s_gs")
        s_hd = sem("s_hd")
        s_dn = sem("s_dn")
        s_oA = sem("s_oA")
        s_oV = sem("s_oV")
        s_osf = sem("s_osf")
        s_ost = sem("s_ost")
        s_ysl = [sem(f"s_ysl{i}") for i in range(4)]
        s_g5 = sem("s_g5")
        s_fy = sem("s_fy")
        s_f1 = sem("s_f1")
        s_f2 = sem("s_f2")
        s_out = [sem(f"s_out{i}") for i in range(2)]

        block = ctx.enter_context(nc.Block())

        def a_view(slot):
            return raw[:, slot, :].rearrange("p (k n) -> p k n", k=4)

        def w_view(ring, slot):
            return ring[:, slot, :].rearrange("p (k n) -> p k n", k=KC)

        def raw_of(pos):
            return pos % RAW

        def raw_count(idx3, pos):
            return 16 * (idx3 + pos // RAW + 1)

        POS = {x: i for i, x in enumerate(LOADS)}

        def group_raw(g):
            return PRE // RAW + (len(LOADS) // RAW) * g

        @block.sync
        def _(sp):
            ab = t["ada_b"][0].rearrange("(a b) -> a b", b=P)
            cw = t["ssm_conv_w"][0].rearrange("s (a b) -> (s a) b", b=P)
            col = lambda v: v.rearrange("(a b) -> a b", b=P)
            sp.dma_start(prow[0:96, 0, :], ab).then_inc(s_pack, 16)
            sp.dma_start(prow[96:112, 0, :], col(t["c"][0])).then_inc(s_pack, 16)
            sp.dma_start(prow[112:128, 0, :], col(t["c_ctx"])).then_inc(s_pack, 16)
            sp.dma_start(xrows[:, 0:2, :], t["x"][0].rearrange("(t p) d -> p t d", p=P)).then_inc(s_x, 16)
            sp.dma_start(xrows[:, 2:4, :], t["ctx"][0].rearrange("(t p) d -> p t d", p=P)).then_inc(s_x, 16)
            sp.dma_start(prow[0:96, 1, :], cw[0:96, :]).then_inc(s_pack, 16)
            sp.dma_start(prow[96:112, 1, :], col(t["norm_g"][0, 0])).then_inc(s_pack, 16)
            sp.dma_start(prow[112:128, 1, :], col(t["norm_g"][0, 1])).then_inc(s_pack, 16)
            sp.dma_start(prow[0:48, 2, :], cw[96:144, :]).then_inc(s_pack, 16)
            sp.dma_start(prow[48:96, 2, :], col(t["ssm_conv_b"][0])).then_inc(s_pack, 16)
            sp.dma_start(prow[96:128, 2, :], col(t["ssm_norm_g"][0])).then_inc(s_pack, 16)
            sp.dma_start(dtb[:, :], t["ssm_dt_bias"][0].rearrange("a (h o) -> (a h) o", o=1)).then_inc(s_pack, 16)
            sp.dma_start(alog[:, :], t["ssm_a_log"][0].rearrange("a (h o) -> (a h) o", o=1)).then_inc(s_pack, 16)
            dd = t["ssm_d"][0].rearrange("(c two) -> two c", two=2)
            with nc.allow_non_contiguous_dma(reason="64 values"):
                sp.dma_start(dcol[0:64, :], dd[0].partition_broadcast(64)).then_inc(s_pack, 16)
                sp.dma_start(dcol[64:128, :], dd[1].partition_broadcast(64)).then_inc(s_pack, 16)
            for a in range(ADA1):
                if a >= RAW:
                    sp.wait_ge(s_ada, a - RAW + 1)
                sp.dma_start(a_view(a % RAW), ada_tile(a // 4, a % 4)).then_inc(s_raw[a % RAW], 16)
            sp.wait_ge(s_ada, ADA1 - RAW + 1)
            sp.dma_start(w_view(raw, ADA1 % RAW), w_in[:, :, DT0:DT0 + P]).then_inc(s_raw[ADA1 % RAW], 16)

            def slot_free(g, pos, first):
                if pos >= RAW:
                    (kind, n), bg = LOADS[pos - RAW], g
                elif not first:
                    (kind, n), bg = LOADS[pos - RAW + len(LOADS)], g - 1
                elif pos < RAW - 1:
                    sp.wait_ge(s_ada, ADA1 - (RAW - 1) + pos + 1)
                    return
                else:
                    sp.wait_ge(s_lo, 1)
                    return
                if kind == "w":
                    sp.wait_ge(s_lo, NCH * bg + (n + 2))
                else:
                    sp.wait_ge(s_ada2, NADA * bg + (n + 1))

            def group_loads(g, first=False):
                for pos, (kind, n) in enumerate(LOADS):
                    slot_free(g, pos, first)
                    if kind == "w" and CHUNKS[n] == ("z", 0):
                        src = w_in[:, :, bass.ds(g * 256 + g * 256, P)]
                    elif kind == "w":
                        src = w_in[:, :, bass.ds(w_in_at(g, n), P)]
                    else:
                        src = ada_tile(2 * g + (NB1 + n // 4), n % 4)
                    sp.dma_start(a_view(raw_of(pos)) if kind == "a" else w_view(raw, raw_of(pos)), src).then_inc(s_raw[raw_of(pos)], 16)

            group_loads(0, first=True)
            with sp.Fori(1, GROUPS) as g:
                group_loads(g)

            def y_load(g):
                for i in range(2):
                    sp.wait_ge(s_yst[i], 16 * 2 * (g + 1) + 16)
                sp.dma_start(yraw[:, GC * g:GC * g + GC, :],
                             y_d[512 * g:512 * g + 512, :].rearrange("(c p) t -> p c t", p=P)).then_inc(s_yld[g], 16)

            sp.wait_ge(s_ads, 16 * 2 * GROUPS)
            sp.dma_start(arow[0:ADA2, 0:P], mod2_d.rearrange("a (b p) -> (a b) p", p=P)).then_inc(s_a2in, 16)
            sp.wait_ge(s_win, M_OUT)
            for g in range(GROUPS - 1):
                y_load(g)
            for k in range(IC):
                if k < RAW:
                    bk, bn = LOADS[len(LOADS) - RAW + k]
                    if bk == "w":
                        sp.wait_ge(s_lo, NCH * (GROUPS - 1) + bn + 2)
                    else:
                        sp.wait_ge(s_ada2, NADA * (GROUPS - 1) + bn + 1)
                else:
                    sp.wait_ge(s_lo, M_OUT + k - RAW + 1)
                sp.dma_start(raw[:, (OUT0 + k) % RAW, :], w_out[k]).then_inc(s_raw[(OUT0 + k) % RAW], 16)
                if k == 2:
                    y_load(GROUPS - 1)
                    sp.wait_ge(s_fin2, IC)
                    sp.dma_start(rw[:, :, 0:NG], t["moe_w_group"][0].rearrange("(k p) n -> p k n", p=P)).then_inc(s_rwl, 16)
                    sp.dma_start(rw[:, :, NG:NG + NE], t["moe_w_expert"][0].rearrange("(k p) n -> p k n", p=P)).then_inc(s_rwl, 16)
                    sp.dma_start(rbias[:, 0:NG], t["moe_b_group"][0].partition_broadcast(P)).then_inc(s_rwl, 16)
                    sp.dma_start(rbias[:, NG:NG + NE], t["moe_b_expert"][0].partition_broadcast(P)).then_inc(s_rwl, 16)
            sp.wait_ge(s_yl, IC)
            sp.wait_ge(s_yss, IC)
            sp.dma_start(x1[:, :, :], t["x"][0].rearrange("(t p) d -> p t d", p=P)).then_inc(s_xres, 16)

            def quarter(src, c):
                sp.dma_start(wr[c % RING][:, :, :], src[:, :, QW * (c % 4):QW * (c % 4) + QW, :].rearrange("o p c n -> (o p) c n")
                             ).then_inc(s_wr[c % RING], 16)

            sp.wait_ge(s_wo, IC)
            for c in range(RING):
                if c == 4:
                    sp.wait_ge(s_x1, 4 * TT)
                quarter((w_gate, w_up)[c // 4][0:1], c)
            sp.wait_ge(s_tab, 1)
            nblk = sp.value_load(itab[0:1, 2 * P:2 * P + 1], min_val=1, max_val=P)
            with sp.Fori(0, nblk) as b:
                e = sp.value_load(itab[0:1, bass.ds(b, 1)], min_val=0, max_val=NE - 1)
                for c in range(RING, NQ):
                    sp.wait_ge(s_el, b * NH + (EL0 + 2 * (c - RING) + 2))
                    quarter((w_gate, w_up)[c // 4][bass.ds(e, 1)], c)
                sp.wait_ge(s_xg, KC)
                sp.wait_ge(s_gTp, 2)
                sp.wait_ge(s_dn, b * FC + 1)
                for f in DOWN_ORDER:
                    sp.dma_start(wd[:, f, :], w_down[bass.ds(e, 1), :, f:f + 1, :].rearrange("o p f n -> (o p) (f n)")).then_inc(s_wd[f], 16)
                after = sp.value_load(itab[0:1, bass.ds(b + 1, 1)], min_val=0, max_val=NE - 1)
                for c in range(RING):
                    sp.wait_ge(s_el, b * NH + (EL0 + 2 * (c + (RING if c < NQ - RING else 0)) + 2))
                    quarter((w_gate, w_up)[c // 4][bass.ds(after, 1)], c)
            sp.wait_ge(s_el, nblk * NH + (EL0 + 4))
            for i in range(NQ - RING):
                sp.wait_ge(s_wr[i], nblk * 32 + 16)
            sp.dma_start(gate5_b[:, :], mod_d[3 * KC:4 * KC, :].rearrange("a b -> (a b)").partition_broadcast(P)).then_inc(s_g5, 16)
            for i in range(NQ - RING, RING):
                sp.wait_ge(s_wr[i], nblk * 16 + 16)
            sp.wait_ge(s_ost, nblk * 16)
            for i in range(4):
                sp.dma_start(ys[:, :, 512 * i:512 * i + 512],
                             rows_d[0:ROWS, 512 * i:512 * i + 512].rearrange("(a p) d -> p a d", p=P)).then_inc(s_ysl[i], 16)
            for q in range(4 * TT):
                nb, tt = q // TT, q % TT
                sp.wait_ge(s_f2, q + 1)
                sp.dma_start(t["out"][0, tt * P:(tt + 1) * P, nb * 512:nb * 512 + 512], fin[:, q % 2, :]).then_inc(s_out[q % 2], 16)
            for i in range(2):
                sp.wait_ge(s_out[i], 16 * 2 * TT)

        @block.gpsimd
        def _(pool):
            pool.memset(ident[:, :], 0.0).then_inc(s_const, 1)
            pool.memset(ones[:, :], 1.0).then_inc(s_const, 1)
            pool.iota(pidx[:, :], pattern=[[0, 1]], base=0, channel_multiplier=1,
                      allow_small_or_imprecise_dtypes=True).then_inc(s_const, 1)
            pool.wait_ge(s_const, 3)
            pool.affine_select(out=ident[:, :], in_=ident[:, :], compare_op=ALU.not_equal, fill=1.0, base=0,
                               pattern=[[-1, P]], channel_multiplier=1).then_inc(s_const, 1)
            pool.affine_select(out=tri_up[:, :], in_=ones[:, :], compare_op=ALU.is_ge, fill=0.0, base=0,
                               pattern=[[1, P]], channel_multiplier=-1).then_inc(s_const, 1)
            pool.affine_select(out=tri_lo[:, :], in_=ones[:, :], compare_op=ALU.is_ge, fill=0.0, base=0,
                               pattern=[[-1, P]], channel_multiplier=1).then_inc(s_const, 1)
            pool.wait_ge(s_cumr, 1)
            for i in range(2):
                rows = slice(HEADS * i, HEADS * (i + 1))
                pool.dma_start(cum_d[rows, :], dtw[rows, 6, 0:L]).then_inc(s_yst[i], 16)
            for i in range(2):
                pool.wait_ge(s_yst[i], 16)

            def load_bc(s, hf):
                for d in range(2):
                    src = cum_d[bass.ds(R * s + (d * HEADS + HALF * hf), HALF), :].rearrange("a b -> (a b)").partition_broadcast(P)
                    dst = bc[:, d * HALF:(d + 1) * HALF, :].rearrange("p a b -> p (a b)")
                    pool.dma_start(dst, src).then_inc(s_bc, 16)

            def group_io(s):
                pool.wait_ge(s_seg, 2 * s + 1)
                pool.wait_ge(s_ebc, 2 * s + 1)
                load_bc(s, 1)
                for c in range(GC):
                    pool.wait_ge(s_fin2, GC * s + c + 1)
                    pool.dma_start(y_d[bass.ds(512 * s + P * c, P), :], ybuf[:, c % 2, :]).then_inc(s_yst[c % 2], 16)

            load_bc(0, 0)
            with pool.Fori(0, GROUPS - 1) as s:
                group_io(s)
                pool.wait_ge(s_seg, 2 * s + 2)
                pool.wait_ge(s_ebc, 2 * s + 2)
                load_bc(s + 1, 0)
            group_io(GROUPS - 1)

            pool.wait_ge(s_a2r, 1)
            pool.dma_start(mod_d[:, :], a2row[:, :]).then_inc(s_mod, 16)
            pool.wait_ge(s_mod, 16)
            pool.wait_ge(s_fin2, IC)
            for i, dst in enumerate((gate_b, shift_b, scale_b)):
                pool.dma_start(dst[:, :], mod_d[KC * i:KC * i + KC, :].rearrange("a b -> (a b)").partition_broadcast(P)).then_inc(s_modb, 16)
            for k in range(IC):
                if k % GC == 0:
                    pool.wait_ge(s_yld[k // GC], 16)
                if k == 0:
                    pool.tensor_tensor(ysq[:, 1, :], yraw[:, 0, :], yraw[:, 0, :], ALU.mult).then_inc(s_yss, 1)
                    continue
                pool.wait_ge(s_yss, k)
                pool.tensor_tensor(ysq[:, 0, :], yraw[:, k, :], yraw[:, k, :], ALU.mult).then_inc(s_ysq, 1)
                pool.wait_ge(s_ysq, k)
                pool.tensor_tensor(ysq[:, 1, :], ysq[:, 1, :], ysq[:, 0, :], ALU.add).then_inc(s_yss, 1)
            pool.wait_ge(s_wo, IC)
            pool.iota(iota_r[:, :], pattern=[[1, RPAD]], base=0, channel_multiplier=0,
                      allow_small_or_imprecise_dtypes=True).then_inc(s_iota, 1)
            pool.iota(iota_e[:, :], pattern=[[1, NE]], base=0, channel_multiplier=0,
                      allow_small_or_imprecise_dtypes=True).then_inc(s_iota, 1)
            pool.affine_select(out=strict[:, :], in_=ones[:, :], compare_op=ALU.is_gt, fill=0.0, base=0,
                               pattern=[[1, P]], channel_multiplier=-1).then_inc(s_iota, 1)
            pool.memset(xgT[:, :, ROWS:RPAD], 0.0).then_inc(s_iota, 1)
            pool.wait_ge(s_tab, 1)
            nblk = pool.value_load(itab[0:1, 2 * P:2 * P + 1], min_val=1, max_val=P)
            pool.sem_inc(s_osf, 1)
            with pool.Fori(0, nblk) as b:
                start = pool.value_load(itab[0:1, bass.ds(b + P, 1)], min_val=0, max_val=ROWS)
                pool.wait_ge(s_oA, b + 2)
                pool.wait_ge(s_oV, b + 2)
                pool.dma_start(rows_d[bass.ds(start, SLOTS), :], osb[:, :]).then_inc(s_ost, 16)
                pool.wait_ge(s_ost, b * 16 + 16)
                pool.sem_inc(s_osf, 1)

        @block.scalar
        def _(act):
            act.wait_ge(s_pk, 1)
            act.activation(cth[:, :, :], cvec[:, :, :], ACT.Tanh).then_inc(s_cth, 1)
            act.wait_ge(s_x, 32)
            for tt in range(4):
                if tt > 0:
                    act.wait_ge(s_ssq, tt)
                act.activation(sqr0[:, :], xrows[:, tt, :], ACT.Square, accum_out=ssq[:, tt:tt + 1]).then_inc(s_ssq, 1)
            act.wait_ge(s_mean, 1)
            act.activation(rms[:, 0:4], ssq[:, 4:8], ACT.Sqrt).then_inc(s_rms, 1)
            act.wait_ge(s_rstd, 1)
            for tt in range(4):
                act.activation(xrows[:, tt, :], xrows[:, tt, :], ACT.Copy, scale=rstd[:, tt:tt + 1]).then_inc(s_xn, 1)
            for blk in range(NB1):
                act.wait_ge(s_a1e, blk + 1)
                act.dma_start(mod1_d[:, 512 * blk:512 * blk + 512], a1rows[:, blk, :]).then_inc(s_a1s, 16)
            act.wait_ge(s_a1s, 16 * NB1)
            act.dma_start(a1in[:, :], mod1_d.rearrange("s (a p) -> (s a) p", p=P)).then_inc(s_a1l, 16)
            for k in range(KC):
                act.wait_ge(s_h, 2 * k + 2)
                act.activation(hTh[:, k, :], xnT[:, k, :], ACT.Copy).then_inc(s_hh, 1)

            def conv_hi(g, n):
                m = NCH * g + (n + 1)
                pos = POS[("w", n)]
                act.wait_ge(s_raw[raw_of(pos)], raw_count(group_raw(g), pos))
                if not (isinstance(g, int) and g == 0 and n == 0):
                    act.wait_ge(s_win, m - 1)
                act.activation(whi[:, (n + 1) % 2, :], raw[:, raw_of(pos), :], ACT.Copy).then_inc(s_hi, 1)

            act.wait_ge(s_raw[ADA1 % RAW], 16 * (ADA1 // RAW + 1))
            act.activation(whi[:, 0, :], raw[:, ADA1 % RAW, :], ACT.Copy).then_inc(s_hi, 1)
            conv_hi(0, 0)
            act.wait_ge(s_dtx, 1)
            act.activation(dtw[:, 1, :], dtw[:, 0, :], ACT.Abs).then_inc(s_dabs, 1)
            act.wait_ge(s_dabs, 1)
            act.activation(dtw[:, 1, :], dtw[:, 1, :], ACT.Exp, scale=-1.0).then_inc(s_dexp, 1)
            act.wait_ge(s_pack, 16 * 13)
            act.activation(arate[:, :], alog[:, :], ACT.Exp).then_inc(s_dexp, 1)
            act.wait_ge(s_du, 1)
            act.activation(dtw[:, 3, :], dtw[:, 2, :], ACT.Ln).then_inc(s_dln, 1)
            act.wait_ge(s_cumr, 1)
            act.activation(dtw[:, 7, 0:LC], dtw[:, 6, L:T], ACT.Exp, scale=-1.0, bias=tot[:, 0:1]).then_inc(s_dw, 1)

            def tanh_of(g, n):
                w = T if CHUNKS[n][0] in "Bx" else L
                act.wait_ge(s_drain, NCH * g + (n + 1))
                act.activation(th[:, n % 2, 0:w], cv[:, n % 2, 0:w], ACT.Tanh).then_inc(s_th, 1)

            def turn_store(g, n):
                i = TURN_AT[n]
                act.wait_ge(s_T, NTURN * g + (i + 1))
                if n == 0:
                    act.activation(btok[:, :, :], TURN[:, 0:2 * P].rearrange("p (t n) -> p t n", t=2), ACT.Copy).then_inc(s_Tev, 1)
                else:
                    c = CHUNKS[n][1]
                    act.activation(xtok[:, :, P * c:P * c + P], TURN[:, :].rearrange("p (t n) -> p t n", t=4), ACT.Copy).then_inc(s_Tev, 1)

            def decays(s, hf):
                i = 2 * s + (hf + 1)
                act.wait_ge(s_seg, i)
                act.activation(wts[:, :, :], wts[:, :, :], ACT.Exp).then_inc(s_expw, 1)
                act.wait_ge(s_bc, 32 * i)
                if hf == 1:
                    act.wait_ge(s_y, GC * s + 2)
                act.activation(ce[:, :, :], bc[:, :, :], ACT.Exp).then_inc(s_ebc, 1)

            def steps(g, w, ssd):
                s = g - 1
                for n in range(NCH):
                    if w and n in (4, 9):
                        ada_row(g, n // 9)
                    if w and n + 1 < NCH:
                        conv_hi(g, n + 1)
                    if w and n + 1 == NCH:
                        if not (isinstance(g, int) and g == GROUPS - 1):
                            conv_hi(g + 1, 0)
                    if ssd and n in (0, 4):
                        decays(s, n // 4)
                    if n > 0 and w:
                        tanh_of(g, n - 1)
                    if n == 0 and ssd:
                        tanh_of(s, NCH - 1)
                    if w and n in CONV_AT:
                        width = T if CHUNKS[n][0] in "Bx" else L
                        act.wait_ge(s_win, NCH * g + (n + 2))
                        if n >= 2:
                            act.wait_ge(s_prod, NCH * g + (n - 1))
                        elif ssd:
                            act.wait_ge(s_prod, NCH * g + (n - 1))
                        col = conv_col(g, n)
                        act.activation(cv[:, n % 2, 0:width], banks[(n + 1) % 2][:, 0:width], ACT.Identity,
                                       scale=tapc[:, 1, bass.ds(col, 1)], bias=tapc[:, 3, bass.ds(col, 1)]).then_inc(s_cvA, 1)
                    if ssd and n == 0:
                        turn_store(s, 8)
                    if ssd and n == 1:
                        turn_store(s, 9)
                    if ssd and n == 2:
                        act.wait_ge(s_st, s + 1)
                        act.activation(st[:, 0, :], STK[0][:, :], ACT.Copy)
                        act.activation(st[:, 1, :], STK[1][:, :], ACT.Copy).then_inc(s_stev, 1)
                    if w and n in (2, 4, 7):
                        turn_store(g, {2: 0, 4: 2, 7: 5}[n])

            def ada_row(g, j):
                act.wait_ge(s_asum, 2 * g + (j + 1))
                act.activation(arow[0:1, :], ADAK[0:1, :], ACT.Copy).then_inc(s_adaev, 1)
                act.wait_ge(s_adaev, 2 * g + (j + 1))
                act.dma_start(mod2_d[bass.ds(2 * g + j, 1), :], arow[0:1, :]).then_inc(s_ads, 16)

            steps(0, True, False)
            with act.Fori(1, GROUPS - 1) as g:
                steps(g, True, True)
            steps(GROUPS - 1, True, True)
            steps(GROUPS, False, True)

            for k in range(IC):
                if k % GC == 0:
                    act.wait_ge(s_yld[k // GC], 16)
                act.activation(yh[:, k, :], yraw[:, k, :], ACT.Copy, scale=ngcol[:, k:k + 1]).then_inc(s_yh, 1)
                m = M_OUT + k
                act.wait_ge(s_raw[(OUT0 + k) % RAW], 16 * ((OUT0 + k) // RAW + 1))
                if k >= 2:
                    act.wait_ge(s_wo, k - 1)
                act.activation(whi[:, m % 2, :], raw[:, (OUT0 + k) % RAW, :], ACT.Copy).then_inc(s_hi, 1)
            act.wait_ge(s_mean, 2)
            act.activation(rms[:, 4:6], ssq[:, 0:2], ACT.Sqrt).then_inc(s_rms, 1)
            for tt in range(TT):
                act.wait_ge(s_x1, 4 * (tt + 1))
                act.wait_ge(s_ssq, 4 + tt)
                act.activation(sqr1[:, :], x1[:, tt, :], ACT.Square, accum_out=ssq[:, 2 + tt:3 + tt]).then_inc(s_ssq, 1)
            act.wait_ge(s_mean, 3)
            act.activation(rms[:, 6:8], ssq[:, 4:6], ACT.Sqrt).then_inc(s_rms, 1)
            for k in range(1, KC, 2):
                act.wait_ge(s_h2t, k + 1)
                act.activation(h2T[:, k, :], banks[k % 2][:, 0:L], ACT.Copy).then_inc(s_h2tA, 1)
            for tt in range(TT):
                act.activation(h2h[:, tt, :], h2[:, tt, :], ACT.Copy).then_inc(s_h2h, 1)
            for tt in range(TT):
                act.wait_ge(s_gmax, tt + 1)
                act.activation(rt[:, tt, 3, 0:NG], rt[:, tt, 0, 0:NG], ACT.Exp, bias=rt[:, tt, 2, 8:9],
                               accum_out=rt[:, tt, 3, 8:9]).then_inc(s_gexp, 1)
            for tt in range(TT):
                act.wait_ge(s_ediff, tt + 1)
                act.activation(rt[:, tt, 3, 10:11], rt[:, tt, 3, 9:10], ACT.Exp).then_inc(s_eexp, 1)
            for k in range(1, KC, 2):
                act.wait_ge(s_xg, k + 1)
                act.activation(xgT[:, k, 0:ROWS], banks[4 + k % 4][:, :], ACT.Copy).then_inc(s_xgA, 1)

            act.wait_ge(s_tab, 1)
            nblk = act.value_load(itab[0:1, 2 * P:2 * P + 1], min_val=1, max_val=P)

            def hi(b, h):
                c = h // 2
                twice = c % RING < NQ - RING
                act.wait_ge(s_wr[c % RING], b * (32 if twice else 16) + (16 * (c // RING) + 16))
                if not (isinstance(b, int) and h < 4):
                    act.wait_ge(s_gu, b * NH + (h - 3))
                act.activation(eh[:, h % 4, :, :], wr[c % RING][:, HW * (h % 2):HW * (h % 2) + HW, :], ACT.Copy).then_inc(s_eh, 1)

            for h in range(4):
                hi(0, h)
            act.sem_inc(s_oA, 1)
            with act.Fori(0, nblk) as b:
                for h in range(4, 11):
                    hi(b, h)
                act.wait_ge(s_gu, b * NH + 8)
                act.activation(gsb[:, :], banks[0][:, :], ACT.Copy).then_inc(s_gc, 1)
                for h in range(11, NH):
                    hi(b, h)
                act.wait_ge(s_gu, b * NH + 16)
                act.activation(usb[:, :], banks[1][:, :], ACT.Copy).then_inc(s_uc, 1)
                act.wait_ge(s_gt, b + 1)
                act.activation(gtanh[:, :, :].rearrange("p f n -> p (f n)"), banks[2][:, 0:FC * SLOTS], ACT.Tanh, scale=0.5).then_inc(s_th2, 1)
                for h in range(4):
                    hi(b + 1, h)
                act.wait_ge(s_dn, b * FC + (FC + 1))
                act.wait_ge(s_osf, b + 1)
                for i in range(2):
                    ins = act.activation(osb[:, 512 * i:512 * i + 512], banks[4 + i][0:SLOTS, :], ACT.Copy)
                ins.then_inc(s_oA, 1)

        @block.vector
        def _(dve):
            chained = [0]

            def ch(ins):
                chained[0] += 1
                ins.then_inc(s_v, 1)
                dve.wait_ge(s_v, chained[0])

            dve.wait_ge(s_ptr, 1)
            ch(dve.tensor_copy(packs[:, :, :].rearrange("p a b -> p (a b)"), banks[3][:, 0:3 * P]))
            dve.tensor_scalar(tapc[:, 0:2, :], packs[:, 1, 0:96].rearrange("p (a b) -> p a b", a=2), 0.5, None, ALU.mult)
            dve.tensor_scalar(tapc[:, 2:4, :], packs[:, 2, 0:96].rearrange("p (a b) -> p a b", a=2), 0.5, None, ALU.mult)
            dve.tensor_scalar(cvec[:, :, :], packs[:, 0, 96:128].rearrange("p (s k) -> p k s", s=2), 0.5, None,
                              ALU.mult).then_inc(s_pk, 1)
            dve.wait_ge(s_cth, 1)
            dve.scalar_tensor_tensor(cvec[:, :, :], cth[:, :, :], 1.0, cvec[:, :, :], ALU.add, ALU.mult).then_inc(s_cvec, 1)
            dve.wait_ge(s_ssq, 4)
            dve.tensor_scalar(ssq[:, 4:8], ssq[:, 0:4], 1.0 / D, EPS, ALU.mult, ALU.add).then_inc(s_mean, 1)
            dve.wait_ge(s_rms, 1)
            dve.reciprocal(rstd[:, 0:4], rms[:, 0:4]).then_inc(s_rstd, 1)
            for k in range(KC):
                dve.wait_ge(s_xt, k + 1)
                dve.tensor_copy(xnT[:, k, :], banks[k % 2][:, :]).then_inc(s_xte, 1)
            for blk in range(NB1):
                dve.wait_ge(s_ada, 4 * blk + 4)
                dve.tensor_copy(a1rows[:, blk, :], banks[5 + blk % 2][0:2, :]).then_inc(s_a1e, 1)
            dve.wait_ge(s_a1T, 1)
            ch(dve.tensor_tensor(adac[:, :, :], ADAK[:, 0:2 * ADA1].rearrange("p (s a) -> p a s", s=2),
                                 adab[:, 0:ADA1].unsqueeze(2).broadcast_to([P, ADA1, 2]), ALU.add))
            ch(dve.scalar_tensor_tensor(acol[:, :, :], adac[:, KC:2 * KC, :], 1.0,
                                        g0col.unsqueeze(2).broadcast_to([P, KC, 2]), ALU.add, ALU.mult))
            dve.wait_ge(s_xte, KC)
            for k in range(KC):
                for q in range(2):
                    dve.tensor_scalar(xnT[:, k, q * L:(q + 1) * L], xnT[:, k, q * L:(q + 1) * L], acol[:, k, q:q + 1],
                                      adac[:, k, q:q + 1], ALU.mult, ALU.add).then_inc(s_h, 1)
                if k > 0:
                    dve.wait_ge(s_hh, k)
                    dve.tensor_tensor(hTl[:, k - 1, :], xnT[:, k - 1, :], hTh[:, k - 1, :].bitcast(F32), ALU.subtract).then_inc(s_hl, 1)
            dve.wait_ge(s_hh, KC)
            dve.tensor_tensor(hTl[:, KC - 1, :], xnT[:, KC - 1, :], hTh[:, KC - 1, :].bitcast(F32), ALU.subtract).then_inc(s_hl, 1)

            def lo(m, slot, raw_tile, free=True):
                dve.wait_ge(s_hi, m + 1)
                if free:
                    dve.wait_ge(s_win, m - 1)
                dve.tensor_tensor(wlo[:, slot, :], raw_tile, whi[:, slot, :].bitcast(F32), ALU.subtract).then_inc(s_lo, 1)

            def conv_lo(g, n):
                lo(NCH * g + (n + 1), (n + 1) % 2, raw[:, raw_of(POS[("w", n)]), :],
                   free=not (isinstance(g, int) and g == 0 and n == 0))

            lo(0, 0, raw[:, ADA1 % RAW, :], free=False)
            conv_lo(0, 0)
            X, E, U, LN, SP_, LA, CUM, WX = range(8)
            dve.wait_ge(s_win, 1)
            dve.wait_ge(s_pack, 16 * 13)
            dve.tensor_scalar(dtw[:, X, :], banks[0][:, :], dtb[:, 0:1], None, ALU.add).then_inc(s_dtx, 1)
            dve.wait_ge(s_dtx, 1)
            dve.wait_ge(s_dexp, 2)
            dve.tensor_scalar(dtw[:, U, :], dtw[:, E, :], 1.0, None, ALU.add).then_inc(s_du, 1)
            dve.wait_ge(s_du, 1)
            ch(dve.tensor_scalar(dtw[:, SP_, :], dtw[:, U, :], 1.0, None, ALU.is_equal))
            ch(dve.scalar_tensor_tensor(dtw[:, LA, :], dtw[:, U, :], -1.0, dtw[:, SP_, :], ALU.add, ALU.add))
            ch(dve.reciprocal(dtw[:, LA, :], dtw[:, LA, :]))
            dve.wait_ge(s_dln, 1)
            ch(dve.tensor_tensor(dtw[:, LN, :], dtw[:, LN, :], dtw[:, SP_, :], ALU.add))
            ch(dve.tensor_tensor(dtw[:, LN, :], dtw[:, LN, :], dtw[:, LA, :], ALU.mult))
            ch(dve.tensor_tensor(dtw[:, LN, :], dtw[:, LN, :], dtw[:, E, :], ALU.mult))
            ch(dve.scalar_tensor_tensor(dtw[:, SP_, :], dtw[:, X, :], 0.0, dtw[:, LN, :], ALU.max, ALU.add))
            ch(dve.tensor_scalar(dtw[:, LA, :], dtw[:, SP_, :], arate[:, 0:1], -1.0, ALU.mult, ALU.mult))
            ch(dve.memset(dtw[:, U, :], 1.0))
            for a in (0, L):
                dve.tensor_tensor_scan(dtw[0:64, CUM, a:a + L], dtw[0:64, U, 0:L], dtw[0:64, LA, a:a + L], 0.0, ALU.mult, ALU.add)
                ch(dve.tensor_tensor_scan(dtw[64:128, CUM, a:a + L][:, ::-1], dtw[64:128, U, 0:L], dtw[64:128, LA, a:a + L][:, ::-1],
                                          0.0, ALU.mult, ALU.add))
            dve.tensor_copy(tot[0:64, :], dtw[0:64, CUM, T - 1:T])
            dve.tensor_copy(tot[64:128, :], dtw[64:128, CUM, L:L + 1]).then_inc(s_cumr, 1)
            dve.wait_ge(s_dw, 1)
            dve.tensor_tensor(dtw[:, WX, 0:LC], dtw[:, WX, 0:LC], dtw[:, SP_, L:T], ALU.mult).then_inc(s_dec, 1)
            dve.wait_ge(s_dtT, 1)
            tk = tokm[:, :, :, :].rearrange("p a d h -> p (a d h)")
            dve.tensor_copy(tk[:, 0:512], banks[3][:, :])
            dve.tensor_copy(tk[:, 512:768], banks[4][:, 0:256]).then_inc(s_tokm, 1)

            def store(g, n):
                kind, c = CHUNKS[n]
                dve.wait_ge(s_th, NCH * g + (n + 1))
                if kind == "C":
                    if not (isinstance(g, int) and g == 0):
                        dve.wait_ge(s_cb, g)
                    dst, w = cT[:, :], L
                elif kind == "z":
                    dst, w = zs[:, c, :], L
                else:
                    i = NTURN * g + TURN_BEFORE[n]
                    if not (isinstance(g, int) and (g == 0 and TURN_BEFORE[n] <= 0)):
                        dve.wait_ge(s_T, i)
                    dst, w = slx[:, n % 2, :], T
                dve.scalar_tensor_tensor(dst, th[:, n % 2, 0:w], 1.0, cv[:, n % 2, 0:w], ALU.add, ALU.mult).then_inc(s_prod, 1)
                if kind == "B":
                    if not (isinstance(g, int) and g == 0):
                        dve.wait_ge(s_cb, g)
                    dve.wait_ge(s_prod, NCH * g + (n + 1))
                    dve.tensor_copy(bT[:, :], slx[:, n % 2, 0:L]).then_inc(s_bT, 1)

            def skip_term(g, n):
                c = CHUNKS[n][1]
                dve.wait_ge(s_prod, NCH * g + (n + 1))
                dve.tensor_scalar(dx[:, c, :], slx[:, n % 2, 0:L], dcol[:, bass.ds(GC * g + c, 1)], None, ALU.mult).then_inc(s_dx, 1)

            def differences(s, hf):
                i = 2 * s + (hf + 1)
                dve.wait_ge(s_bc, 32 * i)
                if hf == 1:
                    dve.wait_ge(s_y, GC * s + 2)
                for d in range(2):
                    for r in range(HALF):
                        q = d * HALF + r
                        j0, j1 = (tokg[:, 2 + j, d, HALF * hf + r:HALF * hf + r + 1] for j in range(2))
                        if d == 0:
                            a, b = (0, 2 * P, 0, L), (2 * P, WC, P, L)
                        else:
                            a, b = (0, P, 0, P), (P, WC, 0, L)
                        for (o0, o1, i0, i1), cj in ((a, j0), (b, j1)):
                            last = dve.tensor_scalar(wts[:, q, o0:o1], bc[:, q, i0:i1], cj, 0.0, ALU.subtract, ALU.min)
                last.then_inc(s_seg, 1)

            def weights(s, hf):
                i = 2 * s + (hf + 1)
                dve.wait_ge(s_expw, i)
                dve.wait_ge(s_cbm, s + 1)
                for d in range(2):
                    w = wts[:, d * HALF:(d + 1) * HALF, :]
                    last = dve.tensor_tensor(w, w, cbm[:, d:d + 1, :].broadcast_to([P, HALF, WC]), ALU.mult)
                last.then_inc(s_wts, 1)
                dve.wait_ge(s_ebc, i)
                dve.wait_ge(s_ct2, s + 1)
                dve.tensor_tensor(ce[:, :, :], ce[:, :, :], cT2[:, :].unsqueeze(1).broadcast_to([P, R, L]), ALU.mult).then_inc(s_ce, 1)

            def scaled_x(s):
                dve.wait_ge(s_Tev, NTURN * s + NTURN)
                dve.wait_ge(s_tg, s + 1)

                def by(k, d):
                    return tokg[:, k:k + 2, d, :].unsqueeze(3).broadcast_to([P, 2, R, 64])

                def heads(v):
                    return v.rearrange("p t (r e) -> p t r e", r=R)

                lat, con = heads(xtok[:, 0:2, :]), heads(xtok[:, 2:4, :])
                dve.tensor_tensor(heads(xdtf[:, :, :]), lat, by(0, 0), ALU.mult)
                dve.tensor_tensor(heads(xwf[:, :, :]), con, by(4, 0), ALU.mult)
                dve.tensor_tensor(lat, lat, by(0, 1), ALU.mult)
                dve.tensor_tensor(con, con, by(4, 1), ALU.mult).then_inc(s_xd, 1)

            def finish(s, c):
                dve.wait_ge(s_y, GC * s + (c + 1))
                dve.wait_ge(s_dx, GC * s + (c + 1))
                dve.wait_ge(s_yst[c % 2], 32 * s + (16 * (c // 2) + 16))
                dve.tensor_tensor(ybuf[:, c % 2, :], banks[6 + c % 2][:, 0:L], dx[:, c, :], ALU.add).then_inc(s_fin1, 1)
                dve.wait_ge(s_fin1, GC * s + (c + 1))
                dve.tensor_tensor(ybuf[:, c % 2, :], ybuf[:, c % 2, :], zs[:, c, :], ALU.mult).then_inc(s_fin2, 1)

            def masked(g):
                dve.wait_ge(s_cb, g + 1)
                c0, c1 = CBK[:, 0:L], CBK[:, L:2 * L]
                dve.tensor_tensor(cbm[:, 0, 0:P], c0[:, 0:P], tri_up[:, :], ALU.mult)
                dve.tensor_copy(cbm[:, 0, P:2 * P], c0[:, P:L])
                dve.tensor_tensor(cbm[:, 0, 2 * P:WC], c1[:, P:L], tri_up[:, :], ALU.mult)
                dve.tensor_tensor(cbm[:, 1, 0:P], c0[:, 0:P], tri_lo[:, :], ALU.mult)
                dve.tensor_copy(cbm[:, 1, P:2 * P], c1[:, 0:P])
                dve.tensor_tensor(cbm[:, 1, 2 * P:WC], c1[:, P:L], tri_lo[:, :], ALU.mult).then_inc(s_cbm, 1)

            def drain(g, n):
                kind = CHUNKS[n][0]
                slot, bank = n % 2, banks[(n + 1) % 2]
                if kind == "z":
                    dve.wait_ge(s_win, NCH * g + (n + 2))
                    dve.tensor_scalar(cv[:, slot, 0:L], bank[:, 0:L], 0.5, None, ALU.mult).then_inc(s_drain, 1)
                    return
                q = 2 if kind in "Bx" else 1
                o = cv[:, slot, 0:q * L].rearrange("p (q t) -> p q t", q=q)
                u = bank[:, 0:q * L].rearrange("p (q t) -> p q t", q=q)
                col = conv_col(g, n)
                i = NCONV * g + (CONV_AT[n] + 1)
                dve.wait_ge(s_cvA, i)
                dve.scalar_tensor_tensor(o[:, :, 1:L], u[:, :, 0:L - 1], tapc[:, 0, bass.ds(col, 1)], o[:, :, 1:L],
                                         ALU.mult, ALU.add).then_inc(s_cvB, 1)
                dve.wait_ge(s_cvB, i)
                dve.scalar_tensor_tensor(o[:, :, 0:L - 1], u[:, :, 1:L], tapc[:, 2, bass.ds(col, 1)], o[:, :, 0:L - 1],
                                         ALU.mult, ALU.add).then_inc(s_drain, 1)

            def steps(g, w, ssd):
                s = g - 1
                for n in range(NCH):
                    if w and n + 1 < NCH:
                        conv_lo(g, n + 1)
                    if w and n + 1 == NCH and not (isinstance(g, int) and g == GROUPS - 1):
                        conv_lo(g + 1, 0)
                    if ssd and n == 0:
                        dve.tensor_copy(tokg[:, :, :, :], tokm[:, :, :, bass.ds(R * s, R)]).then_inc(s_tg, 1)
                        dve.wait_ge(s_prod, NCH * s + 2)
                        dve.tensor_copy(cT2[:, :], cT[:, :]).then_inc(s_ct2, 1)
                        dve.wait_ge(s_tg, s + 1)
                        differences(s, 0)
                    if ssd and n == 4:
                        finish(s, 0)
                        finish(s, 1)
                        differences(s, 1)
                    if ssd and n == 7:
                        finish(s, 2)
                        finish(s, 3)
                    if ssd and n == 0:
                        store(s, NCH - 1)
                        skip_term(s, 8)
                    if w and n > 0:
                        store(g, n - 1)
                    if ssd and n == 1:
                        skip_term(s, 9)
                    if w and n == 4:
                        skip_term(g, 2)
                    if w and n == 7:
                        skip_term(g, 5)
                    if ssd and n in (1, 5):
                        weights(s, n // 5)
                    if w and n == 8:
                        masked(g)
                    if w and n in ADA_STEP:
                        ada_tile_sum(g, ADA_STEP[n])
                    if w:
                        drain(g, n)
                    if ssd and n == 1:
                        scaled_x(s)

            def ada_tile_sum(g, n):
                pos = POS[("a", n)]
                dve.wait_ge(s_raw[raw_of(pos)], raw_count(group_raw(g), pos))
                if n % 4 == 0 and not (isinstance(g, int) and g == 0 and n == 0):
                    dve.wait_ge(s_ads, 32 * g + 4 * n)
                for i in range(4):
                    rows, ck = a_view(raw_of(pos))[:, i, :], cvec[:, 4 * (n % 4) + i, 0:1]
                    if n % 4 == 0 and i == 0:
                        last = dve.tensor_scalar(arow[:, :], rows, ck, None, ALU.mult)
                    else:
                        dve.wait_ge(s_acc, 32 * g + (4 * n + i))
                        last = dve.scalar_tensor_tensor(arow[:, :], rows, ck, arow[:, :], ALU.mult, ALU.add)
                    last.then_inc(s_acc, 1)
                dve.wait_ge(s_acc, 32 * g + (4 * n + 4))
                dve.sem_inc(s_ada2, 1)

            dve.wait_ge(s_tokm, 1)
            dve.wait_ge(s_const, 6)
            steps(0, True, False)
            with dve.Fori(1, GROUPS - 1) as g:
                steps(g, True, True)
            steps(GROUPS - 1, True, True)
            steps(GROUPS, False, True)

            dve.wait_ge(s_a2p, 1)
            ch(dve.tensor_tensor(ada2[:, :], banks[3][:, 256:256 + ADA2], adab[:, ADA1:ADA1 + ADA2], ALU.add))
            dve.tensor_copy(a2c[:, :], ada2[:, :]).then_inc(s_a2, 1)
            dve.wait_ge(s_a2, 1)
            dve.scalar_tensor_tensor(a2c[:, 2 * KC:3 * KC], ada2[:, 2 * KC:3 * KC], 1.0, g1col, ALU.add, ALU.mult).then_inc(s_a2, 1)
            dve.wait_ge(s_a2T, 1)
            dve.tensor_copy(a2row[:, :], banks[3][0:ADA2, 0:P]).then_inc(s_a2r, 1)
            for k in range(IC):
                dve.wait_ge(s_yh, k + 1)
                dve.scalar_tensor_tensor(yl[:, k, :], yraw[:, k, :], ngcol[:, k:k + 1], yh[:, k, :].bitcast(F32),
                                         ALU.mult, ALU.subtract).then_inc(s_yl, 1)
                m = M_OUT + k
                dve.wait_ge(s_hi, m + 1)
                if k >= 2:
                    dve.wait_ge(s_wo, k - 1)
                dve.tensor_tensor(wlo[:, m % 2, :], raw[:, (OUT0 + k) % RAW, :], whi[:, m % 2, :].bitcast(F32),
                                  ALU.subtract).then_inc(s_lo, 1)
            dve.wait_ge(s_wo, IC)
            dve.wait_ge(s_modb, 48)
            dve.wait_ge(s_yss, IC)
            for q in range(8):
                tt, nb = q // 4, slice(q % 4 * 512, q % 4 * 512 + 512)
                dve.tensor_tensor(h2[:, tt, nb], banks[q][:, :], gate_b[:, nb], ALU.mult).then_inc(s_x1a, 1)
                if q == 3:
                    dve.wait_ge(s_yt, 1)
                    dve.tensor_scalar(ssq[:, 0:2], banks[0][:, 0:2], 1.0 / DI, EPS, ALU.mult, ALU.add).then_inc(s_mean, 1)
            dve.wait_ge(s_rms, 2)
            dve.reciprocal(rstd[:, 4:6], rms[:, 4:6]).then_inc(s_rstd, 1)
            dve.wait_ge(s_rstd, 2)
            dve.wait_ge(s_x1a, 8)
            dve.wait_ge(s_xres, 16)
            for q in range(8):
                tt, nb = q // 4, slice(q % 4 * 512, q % 4 * 512 + 512)
                dve.scalar_tensor_tensor(x1[:, tt, nb], h2[:, tt, nb], rstd[:, 4 + tt:5 + tt], x1[:, tt, nb],
                                         ALU.mult, ALU.add).then_inc(s_x1, 1)
            dve.wait_ge(s_ssq, 6)
            dve.tensor_scalar(ssq[:, 4:6], ssq[:, 2:4], 1.0 / D, EPS, ALU.mult, ALU.add).then_inc(s_mean, 1)
            dve.wait_ge(s_rms, 3)
            dve.reciprocal(rstd[:, 6:8], rms[:, 6:8]).then_inc(s_rstd, 1)
            dve.wait_ge(s_rstd, 3)
            for tt in range(TT):
                dve.scalar_tensor_tensor(h2[:, tt, :], x1[:, tt, :], rstd[:, 6 + tt:7 + tt], scale_b[:, :],
                                         ALU.mult, ALU.mult).then_inc(s_h2a, 1)
                dve.wait_ge(s_h2a, tt + 1)
                dve.tensor_tensor(h2[:, tt, :], h2[:, tt, :], shift_b[:, :], ALU.add).then_inc(s_h2, 1)
            for k in range(0, KC, 2):
                dve.wait_ge(s_h2t, k + 1)
                dve.tensor_copy(h2T[:, k, :], banks[k % 2][:, 0:L]).then_inc(s_h2tV, 1)

            dve.wait_ge(s_rwl, 64)
            dve.wait_ge(s_iota, 2)
            for tt in range(TT):
                lg = rt[:, tt, 0:2, :].rearrange("p a b -> p (a b)")
                dve.wait_ge(s_logit, tt + 1)
                ch(dve.tensor_tensor(lg[:, 0:NG + NE], banks[6 + tt][:, 0:NG + NE], rbias[:, :], ALU.add))
                ch(dve.memset(rt[:, tt, 7, 0:8], NEG))
                ch(dve.tensor_copy(rt[:, tt, 7, 0:NG], lg[:, 0:NG]))
                ch(dve.max(rt[:, tt, 2, 0:8], rt[:, tt, 7, 0:8]))
                dve.tensor_scalar(rt[:, tt, 2, 8:9], rt[:, tt, 2, 0:1], -1.0, None, ALU.mult).then_inc(s_gmax, 1)
                ch(dve.max_index(ridx[:, tt, 0, :], rt[:, tt, 2, 0:8], rt[:, tt, 7, 0:8]))
                ch(dve.tensor_copy(rt[:, tt, 6, 2:3], ridx[:, tt, 0, 0:1]))
                ch(dve.tensor_scalar(rt[:, tt, 6, 3:4], rt[:, tt, 6, 2:3], float(EPG), None, ALU.mult))
                ch(dve.tensor_scalar(rt[:, tt, 6, 4:5], rt[:, tt, 6, 3:4], float(EPG), None, ALU.add))
                ch(dve.tensor_scalar(rt[:, tt, 8, :], iota_e[:, :], rt[:, tt, 6, 3:4], None, ALU.is_ge))
                ch(dve.scalar_tensor_tensor(rt[:, tt, 8, :], iota_e[:, :], rt[:, tt, 6, 4:5], rt[:, tt, 8, :], ALU.is_lt, ALU.mult))
                ch(dve.tensor_tensor(rt[:, tt, 4, :], lg[:, NG:NG + NE], rt[:, tt, 8, :], ALU.mult))
                ch(dve.tensor_scalar(rt[:, tt, 9, :], rt[:, tt, 8, :], -NEG, NEG, ALU.mult, ALU.add))
                ch(dve.tensor_tensor(rt[:, tt, 4, :], rt[:, tt, 4, :], rt[:, tt, 9, :], ALU.add))
                ch(dve.max(rt[:, tt, 5, 0:8], rt[:, tt, 4, :]))
                dve.tensor_tensor(rt[:, tt, 3, 9:10], rt[:, tt, 5, 1:2], rt[:, tt, 5, 0:1], ALU.subtract).then_inc(s_ediff, 1)
                ch(dve.max_index(ridx[:, tt, 1, :], rt[:, tt, 5, 0:8], rt[:, tt, 4, :]))
                ch(dve.tensor_copy(rt[:, tt, 6, 0:2], ridx[:, tt, 1, 0:2]))
                for i in range(2):
                    ch(dve.tensor_scalar(pick[:, tt, i, :], iota_e[:, :], rt[:, tt, 6, i:i + 1], None, ALU.is_equal))
                dve.tensor_tensor(pick[:, tt, 2, :], pick[:, tt, 0, :], pick[:, tt, 1, :], ALU.add).then_inc(s_pick, 1)
            for tt in range(TT):
                dve.wait_ge(s_h2h, tt + 1)
                dve.tensor_tensor(h2l[:, tt, :], h2[:, tt, :], h2h[:, tt, :].bitcast(F32), ALU.subtract).then_inc(s_h2, 1)
            CNT, START, NB, BEND, BBEG, OH, OFF, COL, T0 = range(9)
            dve.wait_ge(s_rank, 1)
            ch(dve.memset(rs[:, T0, :], 1.0))
            ch(dve.tensor_copy(rs[:, CNT, :], banks[2][:, 0:NE]))
            ch(dve.tensor_tensor_scan(rs[:, START, :], rs[:, T0, :], rs[:, CNT, :], 0.0, ALU.mult, ALU.add))
            ch(dve.tensor_tensor(rs[:, START, :], rs[:, START, :], rs[:, CNT, :], ALU.subtract))
            ch(dve.tensor_scalar(rs[:, NB, :], rs[:, CNT, :], 0.0, None, ALU.is_gt))
            for q in range(1, L // SLOTS):
                ch(dve.scalar_tensor_tensor(rs[:, NB, :], rs[:, CNT, :], float(q * SLOTS), rs[:, NB, :], ALU.is_gt, ALU.add))
            ch(dve.tensor_scalar(rs[:, NB, 0:1], rs[:, NB, 0:1], 1.0, None, ALU.max))
            ch(dve.tensor_tensor_scan(rs[:, BEND, :], rs[:, T0, :], rs[:, NB, :], 0.0, ALU.mult, ALU.add))
            ch(dve.tensor_tensor(rs[:, BBEG, :], rs[:, BEND, :], rs[:, NB, :], ALU.subtract))
            ch(dve.tensor_scalar(rs[:, OH, :], rs[:, BBEG, :], pidx[:, 0:1], None, ALU.is_le))
            ch(dve.scalar_tensor_tensor(rs[:, OH, :], rs[:, BEND, :], pidx[:, 0:1], rs[:, OH, :], ALU.is_gt, ALU.mult))
            ch(dve.scalar_tensor_tensor(rs[:, OFF, :], rs[:, BBEG, :], -float(SLOTS), rs[:, START, :], ALU.mult, ALU.add))
            ch(dve.tensor_tensor(rs[:, OFF, :], rs[:, OFF, :], rs[:, OH, :], ALU.mult))
            ch(dve.tensor_tensor(rs[:, OH, :], rs[:, OH, :], iota_e[:, :], ALU.mult))
            ch(dve.tensor_reduce(rs[:, COL, 0:1], rs[:, OH, :], AX_X, ALU.add))
            ch(dve.tensor_reduce(rs[:, COL, 3:4], rs[:, OFF, :], AX_X, ALU.add))
            ch(dve.scalar_tensor_tensor(rs[:, COL, 1:2], pidx[:, 0:1], float(SLOTS), rs[:, COL, 3:4], ALU.mult, ALU.add))
            ch(dve.tensor_scalar(rs[:, COL, 1:2], rs[:, COL, 1:2], float(ROWS), None, ALU.min))
            dve.tensor_copy(rs[:, COL, 2:3], rs[:, BEND, NE - 1:NE]).then_inc(s_tabc, 1)
            dve.wait_ge(s_tabr, 1)
            dve.tensor_copy(itab[0:1, :], banks[3][0:1, 0:3 * P]).then_inc(s_tab, 1)
            for tt in range(TT):
                ch(dve.tensor_tensor(rt[:, tt, 7, :], rs[:, START, :], banks[2][:, NE * (tt + 1):NE * (tt + 2)], ALU.add))
                for i in range(2):
                    ch(dve.tensor_tensor(rt[:, tt, 8, :], pick[:, tt, i, :], rt[:, tt, 7, :], ALU.mult))
                    ch(dve.tensor_reduce(rt[:, tt, 6, 8 + i:9 + i], rt[:, tt, 8, :], AX_X, ALU.add))
                ch(dve.tensor_scalar(onehot[:, tt, :], iota_r[:, 0:ROWS], rt[:, tt, 6, 8:9], None, ALU.is_equal))
                dve.scalar_tensor_tensor(onehot[:, tt, :], iota_r[:, 0:ROWS], rt[:, tt, 6, 9:10], onehot[:, tt, :].bitcast(F32),
                                         ALU.is_equal, ALU.add).then_inc(s_place, 1)
            for tt in range(TT):
                dve.wait_ge(s_gexp, tt + 1)
                dve.wait_ge(s_eexp, tt + 1)
                r = rt[:, tt, 3, 10:11]
                ch(dve.scalar_tensor_tensor(rt[:, tt, 10, 0:1], r, 1.0, rt[:, tt, 3, 8:9], ALU.add, ALU.mult))
                ch(dve.reciprocal(rt[:, tt, 10, 1:2], rt[:, tt, 10, 0:1]))
                ch(dve.tensor_tensor(rt[:, tt, 10, 2:3], rt[:, tt, 10, 1:2], r, ALU.mult))
                ch(dve.tensor_scalar(wonehot[:, tt, :], iota_r[:, 0:ROWS], rt[:, tt, 6, 8:9], rt[:, tt, 10, 1:2], ALU.is_equal, ALU.mult))
                ch(dve.tensor_scalar(oh_tmp[:, tt, :], iota_r[:, 0:ROWS], rt[:, tt, 6, 9:10], rt[:, tt, 10, 2:3], ALU.is_equal, ALU.mult))
                dve.tensor_tensor(wonehot[:, tt, :], wonehot[:, tt, :], oh_tmp[:, tt, :], ALU.add).then_inc(s_place, 1)
            for k in range(0, KC, 2):
                dve.wait_ge(s_xg, k + 1)
                dve.tensor_copy(xgT[:, k, 0:ROWS], banks[4 + k % 4][:, :]).then_inc(s_xgV, 1)
            for q in range(2):
                dve.wait_ge(s_gTp, q + 1)
                dve.tensor_copy(gT[:, 2 * q:2 * q + 2, :].rearrange("p a b -> p (a b)"), banks[q][:, :]).then_inc(s_gTv, 1)

            ch(dve.tensor_tensor(stack2[:, :], ident[:, 0:SLOTS], ident[:, SLOTS:2 * SLOTS], ALU.add))
            dve.wait_ge(s_xgA, KC // 2)
            dve.wait_ge(s_xgV, KC // 2)
            dve.wait_ge(s_iota, 4)
            dve.wait_ge(s_tab, 1)
            nblk = dve.value_load(itab[0:1, 2 * P:2 * P + 1], min_val=1, max_val=P)
            start0 = dve.value_load(itab[0:1, P:P + 1], min_val=0, max_val=ROWS)

            def lo(b, h):
                dve.wait_ge(s_eh, b * NH + (h + 1))
                if not (isinstance(b, int) and h < 4):
                    dve.wait_ge(s_gu, b * NH + (h - 3))
                dve.tensor_tensor(el[:, h % 4, :, :].rearrange("p k n -> p (k n)"),
                                  wr[h // 2 % RING][:, HW * (h % 2):HW * (h % 2) + HW, :].rearrange("p k n -> p (k n)"),
                                  eh[:, h % 4, :, :].rearrange("p k n -> p (k n)").bitcast(F32), ALU.subtract).then_inc(s_el, 1)

            def split_rows(b, start):
                dve.tensor_copy(xe[:, :, :], xgT[:, :, bass.ds(start, SLOTS)]).then_inc(s_xe, 1)
                dve.wait_ge(s_xe, b + 1)
                dve.tensor_copy(xs[:, :, 0:SLOTS], xe[:, :, :]).then_inc(s_xh, 1)
                dve.wait_ge(s_xh, b + 1)
                dve.tensor_tensor(xs[:, :, SLOTS:2 * SLOTS], xe[:, :, :], xs[:, :, 0:SLOTS].bitcast(F32), ALU.subtract).then_inc(s_xs, 1)

            dve.sem_inc(s_el, EL0)
            split_rows(0, start0)
            for h in range(4):
                lo(0, h)
            dve.sem_inc(s_oV, 1)
            with dve.Fori(0, nblk) as b:
                after = dve.value_load(itab[0:1, bass.ds(b + (P + 1), 1)], min_val=0, max_val=ROWS)
                for h in range(4, NH):
                    lo(b, h)
                dve.wait_ge(s_th2, b + 1)
                dve.scalar_tensor_tensor(gsil[:, :, :].rearrange("p f n -> p (f n)"), gtanh[:, :, :].rearrange("p f n -> p (f n)"), 1.0,
                                         banks[2][:, 0:FC * SLOTS], ALU.add, ALU.mult).then_inc(s_gs, 1)
                dve.wait_ge(s_ut, b + 1)
                dve.wait_ge(s_gs, b + 1)
                dve.scalar_tensor_tensor(hdn[:, :, :].rearrange("p f n -> p (f n)"), gsil[:, :, :].rearrange("p f n -> p (f n)"), 0.5,
                                         banks[3][:, 0:FC * SLOTS], ALU.mult, ALU.mult).then_inc(s_hd, 1)
                dve.wait_ge(s_gu, b * NH + 16)
                dve.wait_ge(s_xs, b + 1)
                split_rows(b + 1, after)
                for h in range(4):
                    lo(b + 1, h)
                dve.wait_ge(s_dn, b * FC + (FC + 1))
                dve.wait_ge(s_osf, b + 1)
                for i in range(2, 4):
                    ins = dve.tensor_copy(osb[:, 512 * i:512 * i + 512], banks[4 + i][0:SLOTS, :])
                ins.then_inc(s_oV, 1)
            dve.wait_ge(s_g5, 16)
            for q in range(4 * TT):
                nb, tt = slice(q // TT * 512, q // TT * 512 + 512), q % TT
                dve.wait_ge(s_fy, q + 1)
                dve.tensor_tensor(ctmp[:, q % 2, :], banks[q % 4][:, :], gate5_b[:, nb], ALU.mult).then_inc(s_f1, 1)
                dve.wait_ge(s_f1, q + 1)
                if q >= 2:
                    dve.wait_ge(s_out[q % 2], 16 * (q // 2))
                dve.tensor_tensor(fin[:, q % 2, :], ctmp[:, q % 2, :], x1[:, tt, nb], ALU.add).then_inc(s_f2, 1)

        @block.tensor
        def _(pe):
            pe.wait_ge(s_const, 6)
            pe.wait_ge(s_pack, 16 * 13)
            for i in range(3):
                last = pe.transpose(banks[3][:, P * i:P * i + P], prow[:, i, :], ident[:, :])
            last.then_inc(s_ptr, 1)
            for k in range(KC):
                if k >= 2:
                    pe.wait_ge(s_xte, k - 1)
                for tt in range(4):
                    if k == 0:
                        pe.wait_ge(s_xn, tt + 1)
                    last = pe.transpose(banks[k % 2][:, P * tt:P * tt + P], xrows[:, tt, P * k:P * k + P], ident[:, :])
                last.then_inc(s_xt, 1)
            pe.wait_ge(s_cvec, 1)
            for a in range(ADA1):
                pe.wait_ge(s_raw[a % RAW], 16 * (a // RAW + 1))
                blk, q = a // 4, a % 4
                if q == 0 and blk >= 2:
                    pe.wait_ge(s_a1e, blk - 1)
                for i in range(4):
                    k = 4 * q + i
                    last = pe.matmul(banks[5 + blk % 2][0:2, :], cvec[:, k, :], a_view(a % RAW)[:, i, :], start=(k == 0), stop=(k == KC - 1))
                last.then_inc(s_ada, 1)
            pe.wait_ge(s_a1l, 16)
            pe.transpose(ADAK[:, 0:2 * ADA1], a1in[:, :], ident[0:2 * ADA1, 0:2 * ADA1]).then_inc(s_a1T, 1)

            def project(bank, slot, width, inc, k_wait=None):
                wh, wl = w_view(whi, slot), w_view(wlo, slot)
                for k in range(KC):
                    if k_wait:
                        pe.wait_ge(s_hl, k + 1)
                    pe.matmul(bank[:, 0:width], wh[:, k, :], hTh[:, k, 0:width], start=(k == 0), stop=False)
                    pe.matmul(bank[:, 0:width], wh[:, k, :], hTl[:, k, 0:width], start=False, stop=False)
                    last = pe.matmul(bank[:, 0:width], wl[:, k, :], hTh[:, k, 0:width], start=False, stop=(k == KC - 1))
                last.then_inc(inc, 1)

            pe.wait_ge(s_lo, 1)
            project(banks[0], 0, T, s_win, k_wait=True)
            pe.wait_ge(s_dec, 1)
            for i, (q, a) in enumerate(((4, 0), (4, P), (6, 0), (6, P))):
                pe.transpose(banks[3][:, P * i:P * i + P], dtw[:, q, a:a + P], ident[:, :])
            for i in range(2):
                last = pe.transpose(banks[4][:, P * i:P * i + P], dtw[:, 7, P * i:P * i + P], ident[:, :])
            last.then_inc(s_dtT, 1)
            pe.wait_ge(s_tokm, 1)

            def turn(g, n):
                i = NTURN * g + TURN_AT[n]
                pe.wait_ge(s_prod, NCH * g + (n + 1))
                if not (isinstance(g, int) and g == 0 and n == 0):
                    pe.wait_ge(s_Tev, i)
                if n == 0:
                    tiles = [(0, L), (1, L + P)]
                else:
                    tiles = [(q, P * q) for q in range(4)]
                for q, a in tiles:
                    last = pe.transpose(TURN[:, P * q:P * q + P], slx[:, n % 2, a:a + P], ident[:, :])
                last.then_inc(s_T, 1)

            def states(s):
                pe.wait_ge(s_xd, s + 1)
                pe.wait_ge(s_cbm, s + 1)
                for d in range(2):
                    for j in range(2):
                        rhs = xwf[:, j, :] if d == 0 else xtok[:, 2 + j, :]
                        last = pe.matmul(STK[d][:, :], btok[:, j, :], rhs, start=(j == 0), stop=(j == 1))
                last.then_inc(s_st, 1)

            def y_chunk(s, c):
                hf = c // 2
                pe.wait_ge(s_wts, 2 * s + (hf + 1))
                pe.wait_ge(s_ce, 2 * s + (hf + 1))
                pe.wait_ge(s_stev, s + 1)
                if c >= 2:
                    pe.wait_ge(s_fin1, GC * s + (c - 1))
                for r in (2 * c, 2 * c + 1):
                    o = banks[6 + c % 2][64 * (r % 2):64 * (r % 2) + 64, 0:L]
                    hs = slice(64 * r, 64 * r + 64)
                    for d in range(2):
                        q = d * HALF + r % HALF
                        pe.matmul(o, st[:, d, hs], ce[:, q, :], start=(d == 0), stop=False)
                        if d == 0:
                            pe.matmul(o, xdtf[:, 0, hs], wts[:, q, 0:2 * P], start=False, stop=False)
                            pe.matmul(o[:, P:L], xdtf[:, 1, hs], wts[:, q, 2 * P:WC], start=False, stop=False)
                        else:
                            pe.matmul(o[:, 0:P], xtok[:, 0, hs], wts[:, q, 0:P], start=False, stop=False)
                            last = pe.matmul(o, xtok[:, 1, hs], wts[:, q, P:WC], start=False, stop=True)
                last.then_inc(s_y, 1)

            def c_times_b(g):
                pe.wait_ge(s_bT, g + 1)
                pe.wait_ge(s_prod, NCH * g + 2)
                if not (isinstance(g, int) and g == 0):
                    pe.wait_ge(s_stev, g)
                for j in range(2):
                    last = pe.matmul(CBK[:, L * j:L * j + L], bT[:, P * j:P * j + P], cT[:, :], start=True, stop=True)
                last.then_inc(s_cb, 1)

            def steps(g, w, ssd):
                s = g - 1
                for n in range(NCH):
                    if w:
                        m = NCH * g + (n + 1)
                        pe.wait_ge(s_hi, m + 1)
                        pe.wait_ge(s_lo, m + 1)
                        if isinstance(g, int) and g == 0 and n == 0:
                            pass
                        elif isinstance(g, int) and g == 0 and n == 1:
                            pe.wait_ge(s_dtx, 1)
                        else:
                            pe.wait_ge(s_drain, NCH * g + (n - 1))
                        project(banks[(n + 1) % 2], (n + 1) % 2, T if CHUNKS[n][0] in "Bx" else L, s_win)
                    if ssd and n in (0, 1):
                        turn(s, (8, 9)[n])
                    if ssd and n == 2:
                        states(s)
                    if w and n in (2, 4, 7):
                        turn(g, {2: 0, 4: 2, 7: 5}[n])
                    if ssd and n in (3, 6):
                        y_chunk(s, 0 if n == 3 else 2)
                        y_chunk(s, 1 if n == 3 else 3)
                    if w and n == 7:
                        c_times_b(g)
                    if w and n in (3, 8):
                        pe.wait_ge(s_acc, 32 * g + (16 if n == 3 else 32))
                        pe.matmul(ADAK[0:1, :], ones[:, 0:1], arow[:, :], start=True, stop=True).then_inc(s_asum, 1)

            steps(0, True, False)
            with pe.Fori(1, GROUPS - 1) as g:
                steps(g, True, True)
            steps(GROUPS - 1, True, True)
            steps(GROUPS, False, True)

            pe.wait_ge(s_a2in, 16)
            pe.wait_ge(s_Tev, NTURN * GROUPS)
            pe.transpose(banks[3][:, 256:256 + ADA2], arow[0:ADA2, 0:P], ident[0:ADA2, 0:ADA2]).then_inc(s_a2p, 1)
            pe.wait_ge(s_a2, 2)
            pe.transpose(banks[3][0:ADA2, 0:P], a2c[:, :], ident[:, :]).then_inc(s_a2T, 1)
            pe.wait_ge(s_adaev, 2 * GROUPS)
            pe.wait_ge(s_stev, GROUPS)
            pe.wait_ge(s_a2r, 1)
            pe.wait_ge(s_fin1, IC)
            for k in range(IC):
                m = M_OUT + k
                pe.wait_ge(s_yl, k + 1)
                pe.wait_ge(s_lo, m + 1)
                for tt in range(TT):
                    ys_, yls = yh[:, k, P * tt:P * tt + P], yl[:, k, P * tt:P * tt + P]
                    for a, ring, first, final in ((ys_, whi, True, False), (ys_, wlo, False, False), (yls, whi, False, True)):
                        for nb in range(4):
                            last = pe.matmul(banks[4 * tt + nb][:, :], a, ring[:, m % 2, 512 * nb:512 * nb + 512],
                                             start=(k == 0 and first), stop=(k == IC - 1 and final))
                last.then_inc(s_wo, 1)
            pe.wait_ge(s_yss, IC)
            pe.wait_ge(s_x1a, 1)
            for tt in range(TT):
                last = pe.matmul(banks[0][:, tt:tt + 1], ysq[:, 1, P * tt:P * tt + P], ones[:, 0:1], start=True, stop=True)
            last.then_inc(s_yt, 1)
            pe.wait_ge(s_h2, TT)
            for k in range(KC):
                if k >= 2:
                    pe.wait_ge(s_h2tV if k % 2 == 0 else s_h2tA, k // 2)
                for tt in range(TT):
                    last = pe.transpose(banks[k % 2][:, P * tt:P * tt + P], h2[:, tt, P * k:P * k + P], ident[:, :])
                last.then_inc(s_h2t, 1)
            pe.wait_ge(s_rwl, 64)
            pe.wait_ge(s_h2tV, KC // 2)
            pe.wait_ge(s_h2tA, KC // 2)
            for tt in range(TT):
                for k in range(KC):
                    last = pe.matmul(banks[6 + tt][:, 0:NG + NE], h2T[:, k, P * tt:P * tt + P], rw[:, k, :], start=(k == 0), stop=(k == KC - 1))
                last.then_inc(s_logit, 1)
            pe.wait_ge(s_pick, TT)
            pe.wait_ge(s_iota, 3)
            for tt in range(TT):
                pe.matmul(banks[2][:, 0:NE], ones[:, :], pick[:, tt, 2, :], start=(tt == 0), stop=(tt == 1))
            pe.matmul(banks[2][:, NE:2 * NE], strict[:, :], pick[:, 0, 2, :], start=True, stop=True)
            pe.matmul(banks[2][:, 2 * NE:3 * NE], ones[:, :], pick[:, 0, 2, :], start=True, stop=False)
            pe.matmul(banks[2][:, 2 * NE:3 * NE], strict[:, :], pick[:, 1, 2, :], start=False, stop=True).then_inc(s_rank, 1)
            pe.wait_ge(s_tabc, 1)
            for i in range(3):
                last = pe.matmul(banks[3][0:1, P * i:P * i + P], rs[:, 7, i:i + 1], ident[:, :], start=True, stop=True)
            last.then_inc(s_tabr, 1)
            pe.wait_ge(s_place, TT)
            pe.wait_ge(s_h2, 2 * TT)
            for k in range(KC):
                if k >= 4:
                    pe.wait_ge(s_xgV if k % 2 == 0 else s_xgA, (k - 4) // 2 + 1)
                for tt in range(TT):
                    pe.matmul(banks[4 + k % 4][:, :], h2h[:, tt, k:D:KC], onehot[:, tt, :], start=(tt == 0), stop=False)
                    last = pe.matmul(banks[4 + k % 4][:, :], h2l[:, tt, k:D:KC], onehot[:, tt, :], start=False, stop=(tt == TT - 1))
                last.then_inc(s_xg, 1)
            pe.wait_ge(s_place, 2 * TT)
            for q in range(2):
                for i in range(2):
                    for tt in range(TT):
                        last = pe.transpose(banks[q][:, 256 * i + P * tt:256 * i + P * tt + P],
                                            wonehot[:, tt, P * (2 * q + i):P * (2 * q + i) + P], ident[:, :])
                last.then_inc(s_gTp, 1)
            pe.wait_ge(s_gTv, 2)
            pe.wait_ge(s_tab, 1)
            nblk = pe.value_load(itab[0:1, 2 * P:2 * P + 1], min_val=1, max_val=P)
            pe.sem_inc(s_dn, 1)
            with pe.Fori(0, nblk) as b:
                pe.wait_ge(s_xs, b + 1)
                for h in range(NH):
                    pe.wait_ge(s_eh, b * NH + (h + 1))
                    pe.wait_ge(s_el, b * NH + (EL0 + h + 1))
                    for i in range(HW):
                        k = HW * (h % 8) + i
                        pe.matmul(banks[h // 8][:, :], xs[:, k, :], eh[:, h % 4, i, :], start=(k == 0), stop=False)
                        last = pe.matmul(banks[h // 8][:, :], xs[:, k, :], el[:, h % 4, i, :], start=False, stop=(k == KC - 1))
                    last.then_inc(s_gu, 1)
                for copied, src, bank, done in ((s_gc, gsb, banks[2], s_gt), (s_uc, usb, banks[3], s_ut)):
                    pe.wait_ge(copied, b + 1)
                    for f in range(FC):
                        last = pe.matmul(bank[:, SLOTS * f:SLOTS * f + SLOTS], src[:, P * f:P * f + P], stack2[:, :], start=True, stop=True)
                    last.then_inc(done, 1)
                pe.wait_ge(s_hd, b + 1)
                pe.wait_ge(s_oA, b + 1)
                pe.wait_ge(s_oV, b + 1)
                for f in DOWN_ORDER:
                    pe.wait_ge(s_wd[f], b * 16 + 16)
                    for nb in range(4):
                        last = pe.matmul(banks[4 + nb][0:SLOTS, :], hdn[:, f, :], wd[:, f, 512 * nb:512 * nb + 512],
                                         start=(f == DOWN_ORDER[0]), stop=(f == DOWN_ORDER[-1]))
                    last.then_inc(s_dn, 1)
            for q in range(4 * TT):
                nb, tt = q // TT, q % TT
                if tt == 0:
                    pe.wait_ge(s_ysl[nb], 16)
                if q >= 4:
                    pe.wait_ge(s_f1, q - 3)
                for i in range(ROWS // P):
                    last = pe.matmul(banks[q % 4][:, :], gT[:, i, P * tt:P * tt + P], ys[:, i, 512 * nb:512 * nb + 512],
                                     start=(i == 0), stop=(i == ROWS // P - 1))
                last.then_inc(s_fy, 1)


_USED = ["x", "c", "ctx", "c_ctx", "ada_w", "ada_b", "norm_g", "ssm_w_in", "ssm_conv_w", "ssm_conv_b", "ssm_a_log",
         "ssm_dt_bias", "ssm_d", "ssm_norm_g", "ssm_w_out", "moe_w_group", "moe_b_group", "moe_w_expert", "moe_b_expert",
         "moe_w_gate", "moe_w_up", "moe_w_down"]


def kernel(**inputs):
    import numpy as _np
    import concourse.bacc as _bacc
    from concourse import mybir as _mybir
    from concourse.bass_utils import run_bass_kernel_spmd as _run

    nc = _bacc.Bacc("TRN2", target_bir_lowering=False, num_devices=1)
    arrays, t = {}, {}
    for name in _USED:
        a = _np.ascontiguousarray(inputs[name])
        arrays[f"in_{name}"] = a
        t[name] = nc.dram_tensor(f"in_{name}", a.shape, _mybir.dt.from_np(a.dtype), kind="ExternalInput").ap()
    shape = _np.shape(inputs["x"])
    t["out"] = nc.dram_tensor("out_0", shape, _mybir.dt.float32, kind="ExternalOutput").ap()
    build(nc, t)
    r = _run(nc, [arrays], core_ids=[0])
    return r.results[0]["out_0"]
```
